# Optimizing a Trainium2 kernel written in Bass

```python
import math
import jax
import jax.numpy as jnp
from jax import lax
import numpy as np

D_MODEL = 1024
BATCH = 1
SEQ = 256
DEPTH = 2

M_HEADS = 4
M_HEAD_DIM = 128
M_WIDTH = M_HEADS * M_HEAD_DIM
M_CHUNK = 128
CONV_WIDTH = 4
A_HEADS = 8
A_HEAD_DIM = 64
A_WIDTH = A_HEADS * A_HEAD_DIM
MOBA_BLOCK = 256
MOBA_TOPK = 3
Q_CHUNK = 16
REL_BUCKETS = 32
REL_MAX_DIST = 1024
D_FF_DENSE = 2816
N_EXPERTS = 8
TOP_K = 2
D_FF_EXPERT = 3584
N_DENSE = (DEPTH + 1) // 2
N_MOE = DEPTH // 2
EPS = 1e-6

IN_SIZES = (M_WIDTH, M_WIDTH, M_WIDTH, M_WIDTH, M_HEADS, M_HEADS, A_WIDTH, A_WIDTH, A_WIDTH, D_MODEL, D_MODEL)
IN_WIDTH = sum(IN_SIZES)

kernel_name = 'hybrid_mlstm_moba_moe_block'

def rms_norm(x, g):
    x32 = x.astype(jnp.float32)
    y = x32 * lax.rsqrt(jnp.mean(x32 * x32, axis=-1, keepdims=True) + EPS)
    return (y * g.astype(jnp.float32)).astype(x.dtype)

def split_columns(z):
    cuts = []
    acc = 0
    for s in IN_SIZES[:-1]:
        acc += s
        cuts.append(acc)
    return jnp.split(z, cuts, axis=-1)

def causal_depthwise_conv(x, w, b):
    c = x.shape[-1]
    y = lax.conv_general_dilated(x, w[:, None, :].astype(x.dtype), window_strides=(1,),
                                 padding=[(CONV_WIDTH - 1, 0)],
                                 dimension_numbers=('NWC', 'WIO', 'NWC'),
                                 feature_group_count=c)
    return y + b.astype(x.dtype)

def t5_bucket(dist):
    n = jnp.maximum(dist, 0)
    max_exact = REL_BUCKETS // 2
    log_ratio = jnp.log(jnp.maximum(n, max_exact).astype(jnp.float32) / max_exact) / math.log(REL_MAX_DIST / max_exact)
    large = max_exact + (log_ratio * (REL_BUCKETS - max_exact)).astype(jnp.int32)
    large = jnp.minimum(large, REL_BUCKETS - 1)
    return jnp.where(n < max_exact, n, large)

def gather_blocks(blocks, idx):
    return jax.vmap(jax.vmap(lambda bl, ix: bl[ix]))(blocks, idx)

def mlstm_chunkwise(q, k, v, i_pre, f_pre):
    B, S, H, DH = q.shape
    L = M_CHUNK
    NC = S // L
    f32 = jnp.float32

    def chunk(a):
        a = a.astype(f32).reshape((B, NC, L, H) + a.shape[3:])
        return jnp.moveaxis(a, (1, 3), (0, 2))

    qc = chunk(q)
    kc = chunk(k) * (DH ** -0.5)
    vc = chunk(v)
    log_f = chunk(jax.nn.log_sigmoid(f_pre.astype(f32)))
    log_i = chunk(i_pre)
    bcum = jnp.cumsum(log_f, axis=-1)
    causal = jnp.tril(jnp.ones((L, L), dtype=bool))

    def step(carry, xs):
        C, n, m = carry
        qq, kk, vv, bb, ii = xs
        dlog = jnp.where(causal, bb[..., :, None] - bb[..., None, :] + ii[..., None, :], -jnp.inf)
        a = bb + m[..., None]
        mt = jnp.maximum(a, jnp.max(dlog, axis=-1))
        w_intra = jnp.exp(dlog - mt[..., None])
        w_state = jnp.exp(a - mt)
        s = jnp.einsum('bhtd,bhsd->bhts', qq, kk) * w_intra
        num = jnp.einsum('bhts,bhse->bhte', s, vv) + w_state[..., None] * jnp.einsum('bhtd,bhde->bhte', qq, C)
        den = jnp.sum(s, axis=-1) + w_state * jnp.einsum('bhtd,bhd->bht', qq, n)
        h = num / jnp.maximum(jnp.abs(den), jnp.exp(-mt))[..., None]
        b_last = bb[..., -1]
        g = b_last[..., None] - bb + ii
        m_new = jnp.maximum(b_last + m, jnp.max(g, axis=-1))
        decay = jnp.exp(b_last + m - m_new)
        ws = jnp.exp(g - m_new[..., None])
        C = decay[..., None, None] * C + jnp.einsum('bhs,bhsd,bhse->bhde', ws, kk, vv)
        n = decay[..., None] * n + jnp.einsum('bhs,bhsd->bhd', ws, kk)
        return (C, n, m_new), h

    init = (jnp.zeros((B, H, DH, DH), f32), jnp.zeros((B, H, DH), f32), jnp.zeros((B, H), f32))
    _, h = lax.scan(step, init, (qc, kc, vc, bcum, log_i))
    return jnp.moveaxis(h, (0, 2), (1, 3)).reshape(B, S, H, DH)

def moba_attention(q, k, v, rel_bias):
    B, H, S, DA = q.shape
    BS = MOBA_BLOCK
    NB = -(-S // BS)
    SP = NB * BS
    f32 = jnp.float32
    pad = [(0, 0), (0, 0), (0, SP - S), (0, 0)]
    q = jnp.pad(q, pad)
    k = jnp.pad(k, pad)
    v = jnp.pad(v, pad)
    kb = k.reshape(B, H, NB, BS, DA)
    vb = v.reshape(B, H, NB, BS, DA)
    k_mean = jnp.mean(kb.astype(f32), axis=3)
    gate = jnp.einsum('bhsd,bhnd->bhsn', q.astype(f32), k_mean)
    q_blk = jnp.arange(SP) // BS
    past = jnp.arange(NB)[None, :] < q_blk[:, None]
    gate = jnp.where(past, gate, -jnp.inf)
    n_sel = min(MOBA_TOPK, NB)
    _, sel = lax.top_k(gate, n_sel)
    sel_ok = sel < q_blk[:, None]
    nqc = SP // Q_CHUNK

    def by_chunk(a):
        return jnp.moveaxis(a.reshape((B, H, nqc, Q_CHUNK) + a.shape[3:]), 2, 0)

    bias_hb = rel_bias.T
    head_ix = jnp.arange(H)[None, :, None, None, None]
    scale = DA ** -0.5

    def attend(args):
        qq, ss, ok, start = args
        qpos = start + jnp.arange(Q_CHUNK)
        blk = start // BS
        own_k = lax.dynamic_index_in_dim(kb, blk, axis=2, keepdims=False)
        own_v = lax.dynamic_index_in_dim(vb, blk, axis=2, keepdims=False)
        own_pos = blk * BS + jnp.arange(BS)
        sel_k = gather_blocks(kb, ss)
        sel_v = gather_blocks(vb, ss)
        sel_pos = ss[..., None] * BS + jnp.arange(BS)
        l_own = jnp.einsum('bhqd,bhkd->bhqk', qq, own_k).astype(f32) * scale \
            + bias_hb[:, t5_bucket(qpos[:, None] - own_pos[None, :])]
        l_own = jnp.where(own_pos[None, :] <= qpos[:, None], l_own, -jnp.inf)
        l_sel = jnp.einsum('bhqd,bhqnkd->bhqnk', qq, sel_k).astype(f32) * scale \
            + bias_hb[head_ix, t5_bucket(qpos[None, None, :, None, None] - sel_pos)]
        l_sel = jnp.where(ok[..., None], l_sel, -jnp.inf)
        logits = jnp.concatenate([l_own, l_sel.reshape(B, H, Q_CHUNK, n_sel * BS)], axis=-1)
        p = jax.nn.softmax(logits, axis=-1).astype(v.dtype)
        p_own = p[..., :BS]
        p_sel = p[..., BS:].reshape(B, H, Q_CHUNK, n_sel, BS)
        return jnp.einsum('bhqk,bhkd->bhqd', p_own, own_v) + jnp.einsum('bhqnk,bhqnkd->bhqd', p_sel, sel_v)

    starts = jnp.arange(nqc, dtype=jnp.int32) * Q_CHUNK
    out = lax.map(attend, (by_chunk(q), by_chunk(sel), by_chunk(sel_ok), starts))
    out = jnp.moveaxis(out, 0, 2).reshape(B, H, SP, DA)
    return out[:, :, :S]

def hybrid_mixer(h, rel_bias, w_in, conv_w, conv_b, igate_b, fgate_b, mlstm_norm_g,
                 q_norm_g, k_norm_g, w_branch_a, w_branch_b, w_out):
    B, S, _ = h.shape
    z = jnp.einsum('bsd,dp->bsp', h, w_in)
    mq, mk, mv, mo, mi, mf, aq, ak, av, ga, gb = split_columns(z)
    qk = jax.nn.silu(causal_depthwise_conv(jnp.concatenate([mq, mk], axis=-1), conv_w, conv_b))
    mq, mk = jnp.split(qk, 2, axis=-1)

    def heads_m(t):
        return t.reshape(B, S, M_HEADS, M_HEAD_DIM)

    h_cell = mlstm_chunkwise(heads_m(mq), heads_m(mk), heads_m(mv),
                             mi.astype(jnp.float32) + igate_b, mf.astype(jnp.float32) + fgate_b)
    h_cell = jax.nn.sigmoid(heads_m(mo).astype(jnp.float32)) * h_cell
    h_a = rms_norm(h_cell, mlstm_norm_g.reshape(M_HEADS, M_HEAD_DIM)).astype(h.dtype).reshape(B, S, M_WIDTH)
    y_a = h_a @ w_branch_a
    def heads_a(t):
        return t.reshape(B, S, A_HEADS, A_HEAD_DIM).transpose(0, 2, 1, 3)

    qa = rms_norm(heads_a(aq), q_norm_g)
    ka = rms_norm(heads_a(ak), k_norm_g)
    o_b = moba_attention(qa, ka, heads_a(av), rel_bias)
    y_b = o_b.transpose(0, 2, 1, 3).reshape(B, S, A_WIDTH) @ w_branch_b
    y = jax.nn.sigmoid(ga) * y_a + jax.nn.sigmoid(gb) * y_b
    return y @ w_out

def swiglu(h, wg, wu, wd):
    return (jax.nn.silu(h @ wg) * (h @ wu)) @ wd

def moe_swiglu(h, router_w, wg, wu, wd):
    logits = (h @ router_w).astype(jnp.float32)
    top_val, top_idx = lax.top_k(logits, TOP_K)
    top_w = jax.nn.softmax(top_val, axis=-1)
    gates = jnp.sum(jax.nn.one_hot(top_idx, N_EXPERTS, dtype=jnp.float32) * top_w[..., None], axis=-2).astype(h.dtype)
    y = jnp.zeros_like(h)
    for e in range(N_EXPERTS):
        y = y + gates[..., e:e + 1] * swiglu(h, wg[e], wu[e], wd[e])
    return y

def setup_inputs(seed: int = 0) -> dict:
    key = jax.random.key(seed)
    ks = jax.random.split(key, 24)
    f32 = jnp.float32

    def w(k, shape, fan_in):
        return jax.random.normal(k, shape, f32) * (fan_in ** -0.5)

    def gain(k, shape):
        return 1.0 + 0.05 * jax.random.normal(k, shape, f32)

    return {
        'x': jax.random.normal(ks[0], (BATCH, SEQ, D_MODEL), f32),
        'rel_bias': 0.1 * jax.random.normal(ks[1], (REL_BUCKETS, A_HEADS), f32),
        'mix_norm_g': gain(ks[2], (DEPTH, D_MODEL)),
        'w_in': w(ks[3], (DEPTH, D_MODEL, IN_WIDTH), D_MODEL),
        'conv_w': w(ks[4], (DEPTH, CONV_WIDTH, 2 * M_WIDTH), CONV_WIDTH),
        'conv_b': 0.02 * jax.random.normal(ks[5], (DEPTH, 2 * M_WIDTH), f32),
        'igate_b': 0.1 * jax.random.normal(ks[6], (DEPTH, M_HEADS), f32),
        'fgate_b': 3.0 + 3.0 * jax.random.uniform(ks[7], (DEPTH, M_HEADS), f32),
        'mlstm_norm_g': gain(ks[8], (DEPTH, M_WIDTH)),
        'q_norm_g': gain(ks[9], (DEPTH, A_HEAD_DIM)),
        'k_norm_g': gain(ks[10], (DEPTH, A_HEAD_DIM)),
        'w_branch_a': w(ks[11], (DEPTH, M_WIDTH, D_MODEL), M_WIDTH),
        'w_branch_b': w(ks[12], (DEPTH, A_WIDTH, D_MODEL), A_WIDTH),
        'w_out': w(ks[13], (DEPTH, D_MODEL, D_MODEL), D_MODEL),
        'ffn_norm_g': gain(ks[14], (DEPTH, D_MODEL)),
        'dense_w_gate': w(ks[15], (N_DENSE, D_MODEL, D_FF_DENSE), D_MODEL),
        'dense_w_up': w(ks[16], (N_DENSE, D_MODEL, D_FF_DENSE), D_MODEL),
        'dense_w_down': w(ks[17], (N_DENSE, D_FF_DENSE, D_MODEL), D_FF_DENSE),
        'router_w': w(ks[18], (N_MOE, D_MODEL, N_EXPERTS), D_MODEL),
        'expert_w_gate': w(ks[19], (N_MOE, N_EXPERTS, D_MODEL, D_FF_EXPERT), D_MODEL),
        'expert_w_up': w(ks[20], (N_MOE, N_EXPERTS, D_MODEL, D_FF_EXPERT), D_MODEL),
        'expert_w_down': w(ks[21], (N_MOE, N_EXPERTS, D_FF_EXPERT, D_MODEL), D_FF_EXPERT),
    }

def reference(x, rel_bias, mix_norm_g, w_in, conv_w, conv_b, igate_b, fgate_b, mlstm_norm_g,
              q_norm_g, k_norm_g, w_branch_a, w_branch_b, w_out, ffn_norm_g,
              dense_w_gate, dense_w_up, dense_w_down, router_w,
              expert_w_gate, expert_w_up, expert_w_down):
    for layer in range(DEPTH):
        h = rms_norm(x, mix_norm_g[layer])
        x = x + hybrid_mixer(h, rel_bias, w_in[layer], conv_w[layer], conv_b[layer], igate_b[layer],
                             fgate_b[layer], mlstm_norm_g[layer], q_norm_g[layer], k_norm_g[layer],
                             w_branch_a[layer], w_branch_b[layer], w_out[layer])
        h = rms_norm(x, ffn_norm_g[layer])
        j = layer // 2
        if layer % 2 == 0:
            x = x + swiglu(h, dense_w_gate[j], dense_w_up[j], dense_w_down[j])
        else:
            x = x + moe_swiglu(h, router_w[j], expert_w_gate[j], expert_w_up[j], expert_w_down[j])
    return x


_drawn_inputs = setup_inputs


def setup_inputs(seed=0):
    import zlib

    import numpy as np

    out = dict(_drawn_inputs(seed))
    spreads = {}
    factors = {'igate_b': 64.0, 'q_norm_g': 4.535, 'k_norm_g': 3.655}
    for name, (base, spread) in spreads.items():
        noise = np.random.default_rng([zlib.crc32(name.encode()), seed]).standard_normal(out[name].shape)
        drawn = base * np.exp(spread * noise) if base else spread * noise
        out[name] = jnp.asarray(drawn.astype(out[name].dtype))
    for name, factor in factors.items():
        out[name] = (out[name] * factor).astype(out[name].dtype)
    return out
```

```python
from contextlib import ExitStack

import concourse.bass as bass
from concourse import mybir

F32 = mybir.dt.float32
F32R = mybir.dt.float32r
I32 = mybir.dt.int32
ALU = mybir.AluOpType
ACT = mybir.ActivationFunctionType
AX = mybir.AxisListType.X

P = 128
D = 1024
KT = D // P
S = 256
A = S // P
NL = 2
MH, MD = 4, 128
AH, AD = 8, 64
MW, AW = MH * MD, AH * AD
TAPS = 4
FD = 2816
NE, FE = 8, 3584
EPS = 1e-6
NEG = -1e30

UNIT, PIECE = 2048, 1024
RAW = 6
PARTS = 6
AHEAD = 4

COLS = 512
MIX = 60
FFD = FD // COLS * 12 + 6
FFE = FE // COLS * 12
M0 = [0, MIX + FFD]
DN0 = MIX
EX0 = 2 * MIX + FFD
assert EX0 % PARTS == 0 and FFE % PARTS == 0 and FFE // 2 % RAW == 0 and FD % COLS == 256

ROUNDS = 2
JOBS = ROUNDS * NE
CHOOSE = 6

Q0, K0, V0, O0, G0 = 0, MW, 2 * MW, 3 * MW, 4 * MW
AQ0 = G0 + 2 * MH
GA0 = AQ0 + 3 * AW
CHUNK_COLS = [Q0, K0, V0, O0, AQ0, AQ0 + AW, AQ0 + 2 * AW] + [GA0 + COLS * i for i in range(4)]
NCH = len(CHUNK_COLS)

IDENT, TRIU, STRICT, LAST, FLIP, CAUSAL, IOTA, ONES = range(8)
R_MIXG, R_FFNG, R_CONVW, R_CONVB, R_MNG, R_QG, R_KG = 0, 16, 32, 96, 112, 120, 122
NVEC = 124
BT = 384


def ffn_order(widths):
    order, at = [], 0
    n = len(widths)
    for c in range(n + 1):
        for kind, cc in (("gate", c), ("up", c), ("down", c - 1)):
            if 0 <= cc < n and (kind == "down" or c < n):
                pieces = 4 * widths[cc] // COLS
                order.append((kind, cc, at, pieces))
                at += pieces
    return order, at


DENSE_W = [COLS] * (FD // COLS) + [FD % COLS]
EXPERT_W = [COLS] * (FE // COLS)


def program(nc, x_in, rel_bias, mix_norm_g, w_in, conv_w, conv_b, igate_b, fgate_b, mlstm_norm_g,
            q_norm_g, k_norm_g, w_branch_a, w_branch_b, w_out, ffn_norm_g, dense_gate, dense_up, dense_down,
            router_w, expert_gate, expert_up, expert_down, consts, bucket_hot, bucket_mask, bias_rows, out):
    with ExitStack() as ctx:
        def sb(name, shape, dt=F32):
            return ctx.enter_context(nc.sbuf_tensor(name, shape, dt))

        def sem(name):
            return ctx.enter_context(nc.semaphore(name))

        raw = sb("raw", [P, RAW, UNIT])
        w_hi = sb("w_hi", [P, PARTS, PIECE], F32R)
        w_lo = sb("w_lo", [P, PARTS, PIECE], F32R)
        x = sb("x", [P, A, D])
        hT_hi = sb("hT_hi", [P, KT, S], F32R)
        hT_lo = sb("hT_lo", [P, KT, S], F32R)
        g_hi = sb("g_hi", [P, A, D], F32R)
        g_lo = sb("g_lo", [P, A, D], F32R)
        cst = sb("cst", [P, 8, P])
        vec = sb("vec", [P, P])
        toep = sb("toep", [P, AH, S])
        gbias = sb("gbias", [P, NL, 2 * MH])
        small = sb("small", [P, 256])
        rt = sb("rt", [P, 32])
        middle_jobs = sb("middle_jobs", [P, 1], I32)
        narrow_sb = sb("narrow_sb", [8, S])
        eps = sb("eps", [P, 1])
        one = sb("one", [P, 1])
        wg_raw = sb("wg_raw", [P, KT, 8])
        wg_hi = sb("wg_hi", [P, KT, 8], F32R)
        wg_lo = sb("wg_lo", [P, KT, 8], F32R)

        mix = ExitStack()

        def mb(name, shape, dt=F32):
            return mix.enter_context(nc.sbuf_tensor(name, shape, dt))

        conv_in = mb("conv_in", [P, 2 * MH, TAPS - 1 + S])
        qk = mb("qk", [P, 2 * MH, S])
        v = mb("v", [P, A, MW])
        so = mb("so", [P, A, MW])
        aqk = mb("aqk", [P, 2, A, AW])
        av = mb("av", [P, A, AW])
        ga = mb("ga", [P, A, D])
        gb = mb("gb", [P, A, D])
        mix.close()
        ffn = ExitStack()

        def fb(name, shape, dt=F32):
            return ffn.enter_context(nc.sbuf_tensor(name, shape, dt))

        aT_hi = fb("aT_hi", [P, 2, 4, S], F32R)
        aT_lo = fb("aT_lo", [P, 2, 4, S], F32R)
        sg = fb("sg", [P, A, COLS])
        act = fb("act", [P, A, COLS])
        y_hi = fb("y_hi", [P, D], F32R)
        y_lo = fb("y_lo", [P, D], F32R)
        pick = fb("pick", [P, A, P], F32R)
        spread = fb("spread", [P, A, P], F32R)
        keys = fb("keys", [P, A, JOBS])
        gates = fb("gates", [P, A, JOBS])
        ffn.close()

        xn = qk
        xn_v = xn[:].rearrange("p a b -> p (a b)").rearrange("p (a b) -> p a b", a=A)
        civ = conv_in[:].rearrange("p a b -> p (a b)")
        n = MH * (MD + 1)
        kw = civ[:, 0:MH * MD].rearrange("p (h d) -> p h d", h=MH)
        caug, st_sb = [civ[:, MH * MD + n * i:MH * MD + n * (i + 1)].rearrange("p (h d) -> p h d", h=MH)
                       for i in range(2)]
        qaT = civ[:, 0:4 * S].rearrange("p (a b) -> p a b", a=4)
        kaT = civ[:, 4 * S:8 * S].rearrange("p (a b) -> p a b", a=4)
        aqv = aqk[:].rearrange("p a b c -> p (a b c)")
        hot_sb, bmask_sb, brow_sb = aqv[0:32, 0:BT], aqv[0:AH, BT:2 * BT], aqv[0:AH, 2 * BT:3 * BT]
        rb_sb, vec_rows = aqv[0:32, 3 * BT:3 * BT + AH], aqv[:, 10 * P:11 * P]
        L = [aqv[:, 384 * i:384 * (i + 1)] for i in range(2)]
        PT = [aqv[:, 768 + 384 * i:768 + 384 * (i + 1)] for i in range(2)]
        gbv = gb[:].rearrange("p a b -> p (a b)")
        Wt = gbv[:, 0:A * MH * P].rearrange("p (a h s) -> p a h s", a=A, h=MH)
        sT = gbv[:, A * MH * P:2 * A * MH * P].rearrange("p (a h s) -> p a h s", a=A, h=MH)
        ob = v
        haT_hi, haT_lo = [t[:, 0, :].rearrange("p (h s) -> p h s", h=MH) for t in (g_hi, g_lo)]
        obT_hi, obT_lo = [t[:, 1, :].rearrange("p (h s) -> p h s", h=4) for t in (g_hi, g_lo)]

        pA = ctx.enter_context(nc.psum_tensor("pA", [P, 4, 512], F32))
        pB = ctx.enter_context(nc.psum_tensor("pB", [P, 4, 512], F32))

        def block_of(i):
            return cst[:, i, :]

        ident = block_of(IDENT)

        def col(c, n=1):
            return vec[:, c:c + n]

        def bank_as(bank, *dims):
            n = 1
            for d in dims:
                n *= d
            names = "abc"[:len(dims)]
            kw_ = {c: d for c, d in zip(names, dims)}
            return bank[:, 0:n].rearrange(f"p ({' '.join(names)}) -> p {' '.join(names)}", **kw_)

        B0, B1, B2, B3 = [pA[:, i, :] for i in range(4)]
        B4, B5, B6, B7 = [pB[:, i, :] for i in range(4)]

        w_loaded = [sem(f"w_loaded{r}") for r in range(RAW)]
        names = ["w_hi_done", "w_lo_done", "w_used",
                 "in_x0", "in_x1", "in_cst", "in_vec", "in_bias", "in_wg0", "in_wg1", "in_wg2", "stored", "brow_stored",
                 "toep_loaded", "act_chain", "dve_chain",
                 "vec_zero", "vec_psum", "vec_ready", "brow_psum", "brow_ready", "flip_psum", "pads_ready",
                 "rms_ready", "xn_ready", "xT_psum", "hT_hi_done", "hT_lo_done", "wg_hi_done", "wg_lo_done",
                 "x_ready", "lin_evac", "gate_psum", "gate_pre", "soft_ready", "lf_ready", "cum_psum",
                 "diag_ready", "rb_psum", "mu0_ready", "mulast_psum", "exp_args", "w_ready", "conv_ready",
                 "qk_ready", "qk_psum", "s_ready", "sT_psum", "sT_ready", "kt_psum", "kw_ready", "c_psum",
                 "c_ready", "state_psum", "state_ready", "num_psum", "cell_ss", "cell_rms", "ha_ready",
                 "haT_psum", "haT_hi_done", "haT_lo_done", "qkn_ss", "qkn_rms", "qkn_ready", "qaT_psum",
                 "qaT_ready", "lg_psum", "L_ready", "P_ready", "PT_psum", "PT_ready", "o_psum", "o_evac",
                 "obT_hi_done", "obT_psum", "obT_lo_done", "ya_done", "y_ready", "yT_psum",
                 "silu_done", "act_done", "aT_psum", "aT_hi_done", "aT_lo_done", "h_parts",
                 "logit_psum", "route_exp", "route_sel", "sel_ready", "rank_psum", "pick_ready", "slot_psum",
                 "slot_ready", "gather_psum", "xg_hi_done", "xg_lo_done", "y_hi_done", "y_lo_done",
                 "scatter_psum", "added", "yT_hi", "g_hi_done", "choose_chain", "middle_ready", "toep_ready", "narrow_psum", "narrow_rows"]
        s = {n: sem(n) for n in names}

        block = ctx.enter_context(nc.Block())

        def loaded_count(m, j):
            return 16 * (m // 2 // RAW + 1) + 16 * (FFE // 2 // RAW) * j

        def piece_count(m, j):
            return m + 1 + FFE * j

        dense_order, n = ffn_order(DENSE_W)
        assert n == FFD
        expert_order, n = ffn_order(EXPERT_W)
        assert n == FFE

        def ends(order):
            return {(k, c): at + n - 1 for k, c, at, n in order}

        def turns(order):
            at = {}
            for i, (kind, c, start, n) in enumerate(order):
                if kind == "gate" and c > 0:
                    at[c - 1] = start + n // 2 - 1
            (kind, c, start, n) = order[-2]
            at[c + 1] = start + n // 2 - 1
            return at

        def load_middle_jobs(eng):
            eng.wait_ge(s["middle_ready"], 1)
            return eng.value_load(middle_jobs[0:1, 0:1], min_val=NE - 2, max_val=JOBS - 2)

        @block.sync
        def _(sp):
            for a in range(A):
                sp.dma_start(x[:, a, :], x_in[0, P * a:P * (a + 1), :]).then_inc(s[f"in_x{a}"], 16)
            sp.dma_start(cst[:], consts.rearrange("p (b c) -> p b c", b=8)).then_inc(s["in_cst"], 16)

            sp.wait_ge(s["in_vec"], 16 * 9)
            sp.wait_ge(s["in_wg0"], 16)

            def load(u, src, shape, j=0):
                if u >= RAW:
                    sp.wait_ge(s["w_lo_done"], 2 * (u - RAW) + 2 + FFE * j)
                dst = raw[:, u % RAW, :].rearrange("p (k n) -> p k n", k=shape)
                sp.dma_start(dst, src).then_inc(w_loaded[u % RAW], 16)

            def k_major(w, u, c0, cols, j=0):
                wv = w.rearrange("(k p) n -> p k n", p=P)
                kn = UNIT // cols
                for i in range(KT // kn):
                    load(u + i, wv[:, kn * i:kn * (i + 1), c0:c0 + cols], kn, j)

            def n_major(w, u, k0, kn, j=0):
                wv = w.rearrange("(k p) n -> p k n", p=P)
                for i in range(kn // 2):
                    load(u + i, wv[:, k0 + 2 * i:k0 + 2 * i + 2, :], 2, j)

            def feed_forward(order, widths, gate, up, down, m0, j=0):
                for kind, c, at, n in order:
                    u = (m0 + at) // 2
                    if kind == "down":
                        n_major(down, u, 4 * c, widths[c] // P, j)
                    else:
                        k_major(gate if kind == "gate" else up, u, COLS * c, widths[c], j)

            for layer in range(NL):
                for i, c0 in enumerate(CHUNK_COLS):
                    k_major(w_in[layer], (M0[layer] + 4 * i) // 2, c0, COLS)
                u = (M0[layer] + 4 * NCH) // 2
                n_major(w_branch_a[layer], u, 0, 4)
                n_major(w_branch_b[layer], u + 2, 0, 4)
                n_major(w_out[layer], u + 4, 0, 8)
                if layer == 0:
                    feed_forward(dense_order, DENSE_W, dense_gate[0], dense_up[0], dense_down[0], DN0)

            def experts(rnd):
                with sp.Fori(0, NE) as e:
                    gate, up, down = [w[0][bass.ds(e, 1)].rearrange("e k n -> (e k) n")
                                      for w in (expert_gate, expert_up, expert_down)]
                    feed_forward(expert_order, EXPERT_W, gate, up, down, EX0, e + NE * rnd)

            experts(0)
            middle = load_middle_jobs(sp)
            with sp.If(middle > NE):
                experts(1)
            for half in range(2):
                for a in range(A):
                    sp.wait_ge(s["added"], 4 * middle + 5 + 2 * half + a)
                    cols = slice(512 * half, 512 * (half + 1))
                    sp.dma_start(out[0, P * a:P * (a + 1), cols], x[:, a, cols]).then_inc(s["stored"], 16)
            sp.wait_ge(s["stored"], 64)

        @block.gpsimd
        def _(g):
            nc.gpsimd.memset(eps[:], EPS).then_inc(s["pads_ready"], 1)
            nc.gpsimd.memset(one[:], 1.0).then_inc(s["pads_ready"], 1)
            wif = [w_in[layer][:, G0:G0 + 8].rearrange("(k p) n -> p k n", p=P) for layer in range(NL)]
            for layer in range(NL):
                g.dma_start(gbias[:, layer, 0:MH], igate_b[layer].partition_broadcast(P)).then_inc(s["in_bias"], 16)
                g.dma_start(gbias[:, layer, MH:], fgate_b[layer].partition_broadcast(P)).then_inc(s["in_bias"], 16)
            g.dma_start(rb_sb, rel_bias).then_inc(s["in_bias"], 16)
            g.dma_start(hot_sb, bucket_hot).then_inc(s["in_bias"], 16)
            g.dma_start(bmask_sb, bucket_mask).then_inc(s["in_bias"], 16)
            g.wait_ge(s["brow_ready"], 1)
            g.dma_start(bias_rows, brow_sb).then_inc(s["brow_stored"], 16)
            g.wait_ge(s["brow_stored"], 16)
            skew = bass.AP(bias_rows.tensor, 0, [[1, P], [BT, AH], [1, S]])
            g.dma_start(toep[:], skew).then_inc(s["toep_loaded"], 16)
            g.wait_ge(s["wg_lo_done"], 1)
            g.dma_start(wg_raw[:], wif[1]).then_inc(s["in_wg1"], 16)
            g.wait_ge(s["wg_lo_done"], 2)
            g.dma_start(wg_raw[:], router_w[0].rearrange("(k p) n -> p k n", p=P)).then_inc(s["in_wg2"], 16)

        REXP, jcount, kcur, gcur, gslot = rt[:, 0:A], rt[:, 2:3], rt[:, 4:4 + A], rt[:, 6:6 + A], rt[:, 8:9]
        sel_v = rt[:, 16:32].rearrange("p (a e) -> p a e", a=A)

        def sm(c, n):
            return small[:, c:c + n]

        SS, RSTD, RMS = sm(0, A), sm(2, A), sm(4, A)
        PRE = sm(8, 16)
        LF = sm(24, 8)
        NABS, LN1, MINF = sm(32, 8), sm(40, 8), sm(48, 8)
        BC, RR, RMAX = sm(56, 8), sm(64, 8), sm(72, 8)
        MU, ST0, MLAST = sm(80, 8), sm(88, 8), sm(96, 8)
        NMU, EARG, DEN = sm(104, 8), sm(112, 16), sm(128, 8)
        CSS, CRMS = sm(136, 8), sm(144, 8)
        QSS, QRMS = sm(152, 32), sm(184, 32)
        MX, SUMS = sm(216, 16), sm(232, 16)

        @block.tensor
        def _(pe):
            mm = nc.tensor.matmul

            def piece(m, work, j=0):
                pe.wait_ge(s["w_lo_done"], piece_count(m, j))
                hi, lo = w_hi[:, m % PARTS, :], w_lo[:, m % PARTS, :]
                for o, (lh, ll), cols, first, swap in work:
                    for n, (l, r) in enumerate(((lh, hi), (lh, lo), (ll, hi))):
                        r = r[:, cols[0]:cols[1]]
                        ins = mm(o, r if swap else l, l if swap else r, start=first and n == 0, stop=True,
                                 skip_group_check=True)
                ins.then_inc(s["w_used"], 1)

            def left(hi, lo, k, a, n=P):
                return hi[:, k, a * n:(a + 1) * n], lo[:, k, a * n:(a + 1) * n]

            def chunk_piece(m, q, cols, banks, hi, lo, tiles, j=0):
                kn = PIECE // cols
                piece(m, [(banks[a][:, 0:cols], left(hi, lo, kn * q + i, a), (cols * i, cols * (i + 1)),
                           q == 0 and i == 0, False) for i in range(kn) for a in range(tiles)], j)

            def row_piece(m, k, opens, banks, hi, lo, tiles, j=0):
                piece(m, [(banks[a][n], left(hi, lo, k, a), (512 * n, 512 * (n + 1)), opens, False)
                          for a in range(tiles) for n in range(2)], j)

            def turn(o, src, first=True):
                return mm(o, src, ident, is_transpose=True, start=first, stop=True, skip_group_check=True)

            pe.wait_ge(s["in_cst"], 16)
            pe.wait_ge(s["in_vec"], 16 * 9)
            turn(B4[:, 0:P], vec_rows).then_inc(s["vec_psum"], 1)

            def normed_turns(q):
                if q == 0:
                    pe.wait_ge(s["vec_ready"], 1)
                for a in range(A):
                    pe.wait_ge(s["xn_ready"], A * q + a + 1)
                    for b in range(4):
                        for i in range(2):
                            k = 2 * b + i
                            ins = turn(pB[:, b, S * i + P * a:S * i + P * (a + 1)],
                                       xn_v[:, a, P * k:P * (k + 1)], i == 0 and a == 0)
                        if a == A - 1:
                            ins.then_inc(s["xT_psum"], 1)

            def narrow(q, wq):
                pe.wait_ge(s["wg_lo_done"], wq)
                for k in range(KT):
                    pe.wait_ge(s["hT_lo_done"], 4 * q + k // 2 + 1)
                    for n, (l, r) in enumerate(((wg_hi, hT_hi), (wg_hi, hT_lo), (wg_lo, hT_hi))):
                        ins = mm(B0[0:8, 0:S], l[:, k, :], r[:, k, :], start=(k == 0 and n == 0), stop=True,
                                 skip_group_check=True)
                ins.then_inc(s["narrow_psum"], 1)
                pe.wait_ge(s["narrow_rows"], wq)
                for a in range(A):
                    ins = mm(B1[:, 8 * a:8 * a + 8], narrow_sb[:, P * a:P * (a + 1)], ident[0:8, 0:8],
                             is_transpose=True, start=(a == 0), stop=True, skip_group_check=True)
                return ins

            def mixer(layer):
                m0 = M0[layer]
                normed_turns(2 * layer)
                narrow(2 * layer, layer + 1).then_inc(s["gate_psum"], 1)

                def chunks(a, b):
                    for t in range(a, b):
                        i, q = t // 4, t % 4
                        banks = [pA[:, 2 * (i % 2) + n, :] for n in range(2)]
                        if q == 0 and i >= 2:
                            pe.wait_ge(s["lin_evac"], NCH * layer + i - 1)
                        if t == 0:
                            pe.wait_ge(s["gate_pre"], layer + 1)
                        if i < 2:
                            piece(m0 + t, [(banks[f // 2][:, S * (f % 2):S * (f % 2 + 1)],
                                            (hT_hi[:, 2 * q + k, :], hT_lo[:, 2 * q + k, :]),
                                            (COLS * k + P * f, COLS * k + P * (f + 1)),
                                            q == 0 and k == 0 and f % 2 == 0, True)
                                           for k in range(2) for f in range(4)])
                        else:
                            chunk_piece(m0 + t, q, COLS, banks, hT_hi, hT_lo, A)

                chunks(0, 4)
                if layer == 0:
                    pe.wait_ge(s["in_bias"], 16 * 7)
                    mm(B6[0:AH, 0:BT], rb_sb, hot_sb, start=True, stop=True).then_inc(s["brow_psum"], 1)
                pe.wait_ge(s["lf_ready"], layer + 1)
                mm(B5[:, 0:8], block_of(TRIU), LF, start=True, stop=True).then_inc(s["cum_psum"], 1)
                chunks(4, 6)
                pe.wait_ge(s["diag_ready"], layer + 1)
                if layer == 0:
                    pe.wait_ge(s["brow_ready"], 1)
                for a in range(A):
                    ins = mm(pB[:, 2 + a, :], block_of(ONES), Wt[:, a].rearrange("p h s -> p (h s)"),
                             start=True, stop=True)
                ins.then_inc(s["rb_psum"], 1)
                chunks(6, 9)
                pe.wait_ge(s["mu0_ready"], layer + 1)
                mm(B7[:, 0:8], block_of(LAST), ST0, start=True, stop=True).then_inc(s["mulast_psum"], 1)
                chunks(9, 19)
                pe.wait_ge(s["qk_ready"], layer + 1)
                for a in range(A):
                    for h in range(MH):
                        tok = slice(P * a, P * (a + 1))
                        ins = mm(pB[:, a, P * h:P * (h + 1)], qk[:, h, tok], qk[:, MH + h, tok],
                                 start=(h == 0), stop=True, skip_group_check=True)
                    ins.then_inc(s["qk_psum"], 1)
                for h in range(MH):
                    ins = turn(B6[:, P * h:P * (h + 1)], qk[:, MH + h, 0:P], h == 0)
                ins.then_inc(s["kt_psum"], 1)
                chunks(19, 22)
                for a in range(A):
                    pe.wait_ge(s["s_ready"], A * layer + a + 1)
                    for h in range(MH):
                        ins = turn(pB[:, a, P * h:P * (h + 1)], Wt[:, a, h, :], h == 0)
                    ins.then_inc(s["sT_psum"], 1)
                chunks(22, 24)
                pe.wait_ge(s["kw_ready"], layer + 1)
                for h in range(MH):
                    mm(B6[:, P * h:P * (h + 1)], kw[:, h, :], v[:, 0, MD * h:MD * (h + 1)], start=(h == 0), stop=True,
                       skip_group_check=True)
                for h in range(MH):
                    ins = mm(B7[:, h:h + 1], kw[:, h, :], one_col, start=(h == 0), stop=True, skip_group_check=True)
                ins.then_inc(s["c_psum"], 1)
                chunks(24, 25)
                for a in range(A):
                    pe.wait_ge(s["sT_ready"], A * layer + a + 1)
                    for h in range(MH):
                        ins = mm(pB[:, a, MD * h:MD * (h + 1)], sT[:, a, h, :], v[:, a, MD * h:MD * (h + 1)],
                                 start=(h == 0), stop=True, skip_group_check=True)
                    ins.then_inc(s["num_psum"], 1)
                pe.wait_ge(s["c_ready"], layer + 1)
                for h in range(MH):
                    o = pB[:, 2 + h // 2, (MD + 1) * (h % 2):(MD + 1) * (h % 2 + 1)]
                    ins = mm(o, qk[:, h, P:S], caug[:, h, :], start=(h % 2 == 0), stop=True, skip_group_check=True)
                ins.then_inc(s["state_psum"], 1)
                chunks(25, 28)
                pe.wait_ge(s["ha_ready"], layer + 1)
                for b in range(2):
                    for i in range(2):
                        for a in range(A):
                            h = 2 * b + i
                            ins = turn(pB[:, 2 + b, S * i + P * a:S * i + P * (a + 1)], so[:, a, MD * h:MD * (h + 1)],
                                       i == 0 and a == 0)
                    ins.then_inc(s["haT_psum"], 1)
                chunks(28, 29)
                if layer == 0:
                    pe.wait_ge(s["toep_loaded"], 16)
                    pe.wait_ge(s["haT_lo_done"], 2)
                    tv = toep[:].rearrange("p h j -> p (h j)")
                    for n in range(4):
                        ins = mm(pB[:, n, :], block_of(FLIP), tv[:, 512 * n:512 * (n + 1)], start=True, stop=True)
                    ins.then_inc(s["flip_psum"], 1)
                chunks(29, 30)
                if layer == 0:
                    pe.wait_ge(s["toep_ready"], 1)
                pe.wait_ge(s["qkn_ready"], layer + 1)
                pe.wait_ge(s["haT_lo_done"], 2 * layer + 2)
                for w in range(2):
                    for t in range(4):
                        for a in range(A):
                            ins = turn(pB[:, 2 * w + t // 2, S * (t % 2) + P * a:S * (t % 2) + P * (a + 1)],
                                       aqk[:, w, a, P * t:P * (t + 1)], t % 2 == 0 and a == 0)
                    ins.then_inc(s["qaT_psum"], 1)
                chunks(30, 32)

                def logits(h):
                    n = AH * layer + h
                    if h == 0:
                        pe.wait_ge(s["qaT_ready"], 2 * layer + 2)
                    if h >= 2:
                        pe.wait_ge(s["L_ready"], n - 1)
                    lanes = slice(AD * (h % 2), AD * (h % 2 + 1))
                    o = pB[:, h % 2, :]
                    mm(o[:, 0:P], qaT[lanes, h // 2, 0:P], kaT[lanes, h // 2, 0:P], start=True, stop=True,
                       skip_group_check=True)
                    mm(o[:, P:P + S], qaT[lanes, h // 2, P:S], kaT[lanes, h // 2, :], start=False, stop=True,
                       skip_group_check=True).then_inc(s["lg_psum"], 1)

                def turn_probs(h):
                    n = AH * layer + h
                    pe.wait_ge(s["P_ready"], n + 1)
                    if n >= 1:
                        pe.wait_ge(s["PT_ready"], n)
                    for b in range(3):
                        ins = turn(B6[:, P * b:P * (b + 1)], L[h % 2][:, P * b:P * (b + 1)], b == 0)
                    ins.then_inc(s["PT_psum"], 1)

                def weigh(h):
                    n = AH * layer + h
                    pe.wait_ge(s["PT_ready"], n + 1)
                    if h == 4:
                        pe.wait_ge(s["o_evac"], 2 * layer + 1)
                    pt = PT[h % 2]
                    o = bank_as(B7, A, 4, AD)
                    vh = slice(AD * h, AD * (h + 1))
                    mm(o[:, 0, h % 4, :], pt[:, 0:P], av[:, 0, vh], start=(h % 4 == 0), stop=True, skip_group_check=True)
                    mm(o[:, 1, h % 4, :], pt[:, P:2 * P], av[:, 0, vh], start=False, stop=True, skip_group_check=True)
                    mm(o[:, 1, h % 4, :], pt[:, 2 * P:3 * P], av[:, 1, vh], start=False, stop=True,
                       skip_group_check=True).then_inc(s["o_psum"], 1)

                logits(0)
                logits(1)
                chunks(32, 33)
                for h in range(AH):
                    turn_probs(h)
                    chunks(33 + h, 34 + h)
                    if h + 2 < AH:
                        logits(h + 2)
                    weigh(h)
                chunks(41, 43)
                pe.wait_ge(s["o_evac"], 2 * layer + 2)
                for b in range(2):
                    for i in range(2):
                        for a in range(A):
                            t = 2 * b + i
                            ins = turn(pB[:, b, S * i + P * a:S * i + P * (a + 1)], ob[:, a, P * t:P * (t + 1)],
                                       i == 0 and a == 0)
                    ins.then_inc(s["obT_psum"], 1)
                chunks(43, 44)
                t = 44
                for n, (hi, lo, p4, done) in enumerate(((haT_hi, haT_lo, pA, "haT_lo_done"),
                                                        (obT_hi, obT_lo, pB, "obT_lo_done"))):
                    pe.wait_ge(s[done], 2 * layer + 2)
                    if n == 0:
                        pe.wait_ge(s["lin_evac"], NCH * (layer + 1))
                    for k in range(4):
                        row_piece(m0 + t, k, k == 0, [[p4[:, 2 * i + c, :] for c in range(2)] for i in range(A)], hi, lo, A)
                        t += 1
                def turn_y(half):
                    pe.wait_ge(s["y_ready"], 2 * layer + half + 1)
                    for b in range(2):
                        for i in range(2):
                            for a in range(A):
                                k = 4 * half + 2 * b + i
                                ins = turn(pA[:, 2 * half + b, S * i + P * a:S * i + P * (a + 1)],
                                           ga[:, a, P * k:P * (k + 1)], i == 0 and a == 0)
                        ins.then_inc(s["yT_psum"], 1)

                turn_y(0)
                pe.wait_ge(s["y_ready"], 2 * layer + 2)
                for k in range(KT):
                    if k == 1:
                        turn_y(1)
                    pe.wait_ge(s["h_parts"], 4 * layer + k // 2 + 1)
                    row_piece(m0 + t, k, k == 0, [[pB[:, 2 * i + c, :] for c in range(2)] for i in range(A)], hT_hi, hT_lo, A)
                    t += 1

            one_col = one[:]

            mixer(0)

            normed_turns(1)
            ta = turns(dense_order)
            pe.wait_ge(s["hT_lo_done"], 8)
            for kind, c, at, n in dense_order:
                if kind == "gate" and c:
                    pe.wait_ge(s["silu_done"], c)
                if kind == "up" and c:
                    pe.wait_ge(s["act_done"], c)
                    pe.wait_ge(s["aT_lo_done"], 2 * c)
                if kind == "down":
                    pe.wait_ge(s["aT_lo_done"], 2 * c + 2)
                for q in range(n):
                    m = DN0 + at + q
                    if kind == "down":
                        row_piece(m, q, c == 0 and q == 0, [[pB[:, 2 * a + h, :] for h in range(2)] for a in range(A)],
                                  aT_hi[:, c % 2], aT_lo[:, c % 2], A)
                    else:
                        banks = [pA[:, (0 if kind == "gate" else 2) + a, :] for a in range(A)]
                        chunk_piece(m, q, DENSE_W[c], banks, hT_hi, hT_lo, A)
                    for cc, pos in ta.items():
                        if pos == at + q:
                            pe.wait_ge(s["act_done"], cc + 1)
                            for b in range(2):
                                for i in range(2 if DENSE_W[cc] == COLS else 1):
                                    for a in range(A):
                                        k = (2 * b + i) if DENSE_W[cc] == COLS else b
                                        ins = turn(pA[:, 2 + b, S * i + P * a:S * i + P * (a + 1)],
                                                   act[:, a, P * k:P * (k + 1)], i == 0 and a == 0)
                                ins.then_inc(s["aT_psum"], 1)

            mixer(1)

            normed_turns(3)
            narrow(3, 3).then_inc(s["logit_psum"], 1)
            pe.wait_ge(s["hT_lo_done"], 16)
            pe.wait_ge(s["sel_ready"], 1)
            sel = sel_v
            mm(B5[:, 0:8], block_of(STRICT), sel[:, 0, :], start=True, stop=True, skip_group_check=True)
            mm(B5[:, 8:16], block_of(ONES), sel[:, 0, :], start=False, stop=True, skip_group_check=True)
            mm(B5[:, 8:16], block_of(STRICT), sel[:, 1, :], start=False, stop=True, skip_group_check=True)
            for a in range(A):
                ins = mm(B5[:, 16:24], block_of(ONES), sel[:, a, :], start=False, stop=True, skip_group_check=True)
            ins.then_inc(s["rank_psum"], 1)

            te = turns(expert_order)
            NCX = len(EXPERT_W)
            D0 = len(DENSE_W)
            T0 = 2 * D0

            def gather(j):
                pe.wait_ge(s["pick_ready"], j + 1)
                for b in range(2):
                    o = bank_as(pB[:, 1 + b, :], 4, P)
                    for i in range(4):
                        k = 4 * b + i
                        for n, (a, src) in enumerate(((0, g_hi), (1, g_hi), (0, g_lo), (1, g_lo))):
                            ins = mm(o[:, i, :], src[:, a, P * k:P * (k + 1)], pick[:, a, :],
                                     start=(i == 0 and n == 0), stop=True, skip_group_check=True)
                    ins.then_inc(s["gather_psum"], 1)

            def slots(j):
                pe.wait_ge(s["choose_chain"], CHOOSE * j + CHOOSE)
                for a in range(A):
                    turn(B7[:, P * a:P * (a + 1)], pick[:, a, :].bitcast(F32), a == 0)
                for a in range(A):
                    ins = mm(B7[:, S:S + 1], pick[:, a, :].bitcast(F32), gcur[:, a:a + 1], start=False, stop=True,
                             skip_group_check=True)
                ins.then_inc(s["slot_psum"], 1)

            def scatter(j, half, last=False):
                pe.wait_ge(s["y_lo_done"], 2 * j + half + 1)
                if half and not last:
                    pe.wait_ge(s["added"], 4 * j + 2)
                for a in range(A):
                    o = pA[:, a, :] if last else pB[:, 1 + a, :]
                    for n, src in enumerate((y_hi, y_lo)):
                        ins = mm(o, spread[:, a, :], src[:, 512 * half:512 * (half + 1)], start=(n == 0), stop=(n == 1))
                    ins.then_inc(s["scatter_psum"], 1)

            def job(j, first=False, last=False):
                for kind, c, at, n in expert_order:
                    if kind == "gate":
                        pe.wait_ge(s["silu_done"], D0 + NCX * j + c)
                        if c == 0:
                            pe.wait_ge(s["xg_lo_done"], 2 * j + 2)
                    if kind == "up":
                        pe.wait_ge(s["act_done"], D0 + NCX * j + c)
                    if kind == "down":
                        pe.wait_ge(s["aT_lo_done"], T0 + NCX * j + c + 1)
                        if c == 0 and not first:
                            pe.wait_ge(s["y_lo_done"], 2 * j)
                    for q in range(n):
                        m = EX0 + at + q
                        if kind == "down":
                            row_piece(m, q, c == 0 and q == 0, [[B2, B3]], aT_hi[:, c % 2], aT_lo[:, c % 2], 1, j)
                        else:
                            chunk_piece(m, q, COLS, [B0 if kind == "gate" else B1], hT_hi, hT_lo, 1, j=j)
                        for cc, pos in te.items():
                            if pos == at + q:
                                pe.wait_ge(s["act_done"], D0 + NCX * j + cc + 1)
                                pe.wait_ge(s["aT_lo_done"], T0 + NCX * j + cc)
                                for k in range(4):
                                    ins = turn(B4[:, P * k:P * (k + 1)], act[:, 0, P * k:P * (k + 1)], k == 0)
                                ins.then_inc(s["aT_psum"], 1)
                        if at + q == 3 and not first:
                            scatter(j - 1, 0)
                        if at + q == 9 and not first:
                            scatter(j - 1, 1)
                        if at + q == 14:
                            slots(j)
                        if at + q == 71 and not last:
                            pe.wait_ge(s["added"], 4 * j) if not first else None
                            gather(j + 1)

            gather(0)
            job(0, first=True)
            middle = load_middle_jobs(pe)
            with pe.Fori(0, middle) as i:
                job(i + 1)
            job(middle + 1, last=True)
            pe.wait_ge(s["added"], 4 * middle + 4)
            scatter(middle + 1, 0)
            scatter(middle + 1, 1, last=True)

        @block.scalar
        def _(eng):
            f = nc.scalar.activation
            chain = [0]

            def link(ins):
                chain[0] += 1
                ins.then_inc(s["act_chain"], 1)
                eng.wait_ge(s["act_chain"], chain[0])

            nxt = [0]

            cap = [EX0 + FFE + AHEAD]

            def split_to(m_end, j=0):
                while nxt[0] < min(m_end, cap[0]):
                    m = nxt[0]
                    eng.wait_ge(w_loaded[m // 2 % RAW], loaded_count(m, j))
                    if m >= PARTS:
                        eng.wait_ge(s["w_used"], piece_count(m - PARTS, j))
                    f(w_hi[:, m % PARTS, :], raw[:, m // 2 % RAW, PIECE * (m % 2):PIECE * (m % 2 + 1)],
                      ACT.Copy).then_inc(s["w_hi_done"], 1)
                    nxt[0] += 1

            def after(m, j=0):
                split_to(m + 1 + AHEAD, j)
                eng.wait_ge(s["w_used"], piece_count(m, j))

            def rms_pass(q):
                if q == 0:
                    eng.wait_ge(s["pads_ready"], 2)
                for a in range(A):
                    if q == 0:
                        eng.wait_ge(s[f"in_x{a}"], 16)
                    else:
                        eng.wait_ge(s["x_ready"], 4 * (q - 1) + 2 * a + 2)
                    link(f(junk_v[:, a, :], x[:, a, :], ACT.Square, accum_out=SS[:, a:a + 1]))
                    f(RMS[:, a:a + 1], SS[:, a:a + 1], ACT.Sqrt, scale=1.0 / D, bias=eps[:]).then_inc(s["rms_ready"], 1)

            junk_v = xn_v

            def parts_hi(q, g_row):
                for b in range(4):
                    eng.wait_ge(s["xT_psum"], 4 * q + b + 1)
                    if q == 0 and b == 0:
                        eng.wait_ge(s["vec_ready"], 1)
                    for i in range(2):
                        k = 2 * b + i
                        ins = f(hT_hi[:, k, :], pB[:, b, S * i:S * (i + 1)], ACT.Copy, scale=col(g_row + k))
                    ins.then_inc(s["hT_hi_done"], 1)

            def narrow_hi(n, name):
                eng.wait_ge(s[name], 16)
                if n == 1:
                    eng.wait_ge(s["gate_psum"], 1)
                if n == 2:
                    eng.wait_ge(s["gate_psum"], 2)
                f(wg_hi[:], wg_raw[:], ACT.Copy).then_inc(s["wg_hi_done"], 1)

            def mixer(layer):
                m0 = M0[layer]
                if layer == 0:
                    narrow_hi(0, "in_wg0")
                else:
                    rms_pass(2 * layer)
                parts_hi(2 * layer, R_MIXG + KT * layer)
                if layer == 1:
                    narrow_hi(1, "in_wg1")
                split_to(m0 + AHEAD)
                eng.wait_ge(s["gate_pre"], layer + 1)
                link(f(NABS, NABS, ACT.Exp))
                f(LN1, NABS, ACT.Ln, bias=one[:]).then_inc(s["soft_ready"], 1)
                for i in range(2):
                    after(m0 + 4 * i + 3)
                    f(conv_in[:, 4 * i:4 * i + 4, TAPS - 1:],
                      pA[:, 2 * i:2 * i + 2, :].rearrange("p b (f t) -> p (b f) t", f=2),
                      ACT.Copy).then_inc(s["lin_evac"], 1)
                split_to(m0 + 10 + AHEAD)
                eng.wait_ge(s["exp_args"], layer + 1)
                link(f(EARG, EARG, ACT.Exp))
                for a in range(A):
                    for h in range(MH):
                        ins = f(Wt[:, a, h, :], Wt[:, a, h, :], ACT.Exp, bias=NMU[:, MH * a + h:MH * a + h + 1])
                ins.then_inc(s["w_ready"], 1)
                after(m0 + 11)
                f(v[:], pA[:, 0:2, :], ACT.Copy).then_inc(s["lin_evac"], 1)
                after(m0 + 15)
                f(so[:], pA[:, 2:4, :], ACT.Sigmoid).then_inc(s["lin_evac"], 1)
                eng.wait_ge(s["conv_ready"], layer + 1)
                f(qk[:], qk[:], ACT.Silu).then_inc(s["qk_ready"], 1)
                after(m0 + 19)
                if layer == 0:
                    eng.wait_ge(s["brow_stored"], 16)
                f(aqk[:, 0], pA[:, 0:2, :], ACT.Copy).then_inc(s["lin_evac"], 1)
                after(m0 + 21)
                for a in range(A):
                    eng.wait_ge(s["sT_psum"], A * layer + a + 1)
                    f(sT[:, a], bank_as(pB[:, a, :], MH, P), ACT.Copy).then_inc(s["sT_ready"], 1)
                after(m0 + 23)
                f(aqk[:, 1], pA[:, 2:4, :], ACT.Copy).then_inc(s["lin_evac"], 1)
                eng.wait_ge(s["c_psum"], layer + 1)
                f(caug[:, :, 0:MD], bank_as(B6, MH, MD), ACT.Copy)
                f(caug[:, :, MD], B7[:, 0:MH], ACT.Copy).then_inc(s["c_ready"], 1)
                after(m0 + 24)
                eng.wait_ge(s["state_psum"], layer + 1)
                for h in range(MH):
                    o = pB[:, 2 + h // 2, (MD + 1) * (h % 2):(MD + 1) * (h % 2 + 1)]
                    ins = f(st_sb[:, h, :], o, ACT.Copy, scale=EARG[:, h:h + 1])
                ins.then_inc(s["state_ready"], 1)
                split_to(m0 + 26 + AHEAD)
                eng.wait_ge(s["cell_ss"], layer + 1)
                f(CRMS, CSS, ACT.Sqrt, scale=1.0 / MD, bias=eps[:]).then_inc(s["cell_rms"], 1)
                split_to(m0 + 27 + AHEAD)
                eng.wait_ge(s["qkn_ss"], layer + 1)
                f(QRMS, QSS, ACT.Sqrt, scale=1.0 / AD, bias=eps[:]).then_inc(s["qkn_rms"], 1)
                after(m0 + 27)
                f(av[:], pA[:, 0:2, :], ACT.Copy).then_inc(s["lin_evac"], 1)
                for b in range(2):
                    eng.wait_ge(s["haT_psum"], 2 * layer + b + 1)
                    for i in range(2):
                        h = 2 * b + i
                        ins = f(haT_hi[:, h, :], pB[:, 2 + b, S * i:S * (i + 1)], ACT.Copy,
                                scale=col(R_MNG + MH * layer + h))
                    ins.then_inc(s["haT_hi_done"], 1)
                split_to(m0 + 30 + AHEAD)
                for w, (dst, row) in enumerate(((qaT, R_QG), (kaT, R_KG))):
                    eng.wait_ge(s["qaT_psum"], 2 * layer + w + 1)
                    f(dst, pB[:, 2 * w:2 * w + 2, :].rearrange("p b (t c) -> p (b t) c", t=2), ACT.Copy,
                      scale=col(row + layer)).then_inc(s["qaT_ready"], 1)
                split_to(m0 + 33 + AHEAD)

                def gate(i):
                    after(m0 + 4 * i + 3)
                    i2 = i - 7
                    dst = ga if i2 < 2 else gb
                    f(dst[:, :, 512 * (i2 % 2):512 * (i2 % 2 + 1)], pA[:, 2 * (i % 2):2 * (i % 2) + 2, :],
                      ACT.Sigmoid).then_inc(s["lin_evac"], 1)

                for h in range(AH):
                    n = AH * layer + h
                    if h in (1, 5):
                        gate(7 + h // 4)
                    eng.wait_ge(s["L_ready"], n + 1)
                    for t, (c0, c1) in enumerate(((0, P), (P, P + S))):
                        ins = f(L[h % 2][:, c0:c1], L[h % 2][:, c0:c1], ACT.Exp, bias=MX[:, 2 * h + t:2 * h + t + 1],
                                accum_out=SUMS[:, 2 * h + t:2 * h + t + 1])
                    ins.then_inc(s["P_ready"], 1)
                    split_to(m0 + 34 + h + AHEAD)
                    eng.wait_ge(s["PT_psum"], n + 1)
                    if h >= 2:
                        eng.wait_ge(s["o_psum"], n - 1)
                    f(PT[h % 2], B6[:, 0:384], ACT.Copy).then_inc(s["PT_ready"], 1)
                gate(9)
                for b in range(2):
                    split_to(m0 + 43 + AHEAD)
                    eng.wait_ge(s["obT_psum"], 2 * layer + b + 1)
                    f(obT_hi[:, 2 * b:2 * b + 2, :], bank_as(pB[:, b, :], 2, S), ACT.Copy).then_inc(s["obT_hi_done"], 1)
                gate(10)
                split_to(m0 + 52 + AHEAD)
                for b in range(4):
                    eng.wait_ge(s["yT_psum"], 4 * layer + b + 1)
                    f(hT_hi[:, 2 * b:2 * b + 2, :], bank_as(pA[:, b, :], 2, S), ACT.Copy).then_inc(s["yT_hi"], 1)
                after(m0 + MIX - 1)

            eng.wait_ge(s["vec_zero"], 1)
            rows = [(R_MIXG, mix_norm_g.rearrange("l (k p) -> (l k) p", p=P)),
                    (R_FFNG, ffn_norm_g.rearrange("l (k p) -> (l k) p", p=P)),
                    (R_CONVW, conv_w.rearrange("l t (k p) -> (l t k) p", p=P)),
                    (R_CONVB, conv_b.rearrange("l (k p) -> (l k) p", p=P)),
                    (R_MNG, mlstm_norm_g.rearrange("l (k p) -> (l k) p", p=P))]
            for r, src in rows:
                eng.dma_start(vec_rows[r:r + src.shape[0], :], src).then_inc(s["in_vec"], 16)
            for r, src in ((R_QG, q_norm_g), (R_KG, k_norm_g)):
                for half in range(2):
                    eng.dma_start(vec_rows[r:r + NL, AD * half:AD * (half + 1)], src).then_inc(s["in_vec"], 16)
            eng.dma_start(wg_raw[:], w_in[0][:, G0:G0 + 8].rearrange("(k p) n -> p k n", p=P)).then_inc(s["in_wg0"], 16)
            rms_pass(0)
            eng.wait_ge(s["vec_psum"], 1)
            f(vec[:], B4[:, 0:P], ACT.Copy).then_inc(s["vec_ready"], 1)
            mixer(0)

            rms_pass(1)
            parts_hi(1, R_FFNG)
            ta, en = turns(dense_order), ends(dense_order)
            for t in range(FFD):
                for c, w in enumerate(DENSE_W):
                    if t == en["gate", c]:
                        after(DN0 + t)
                        if c:
                            eng.wait_ge(s["act_done"], c)
                        f(sg[:, :, 0:w], pA[:, 0:2, 0:w], ACT.Silu).then_inc(s["silu_done"], 1)
                    if t == ta[c]:
                        after(DN0 + t)
                        for b in range(2):
                            eng.wait_ge(s["aT_psum"], 2 * c + b + 1)
                            k = w // COLS + 1
                            f(aT_hi[:, c % 2, k * b:k * (b + 1), :], bank_as(pA[:, 2 + b, :], k, S),
                              ACT.Copy).then_inc(s["aT_hi_done"], 1)
            after(DN0 + FFD - 1)

            mixer(1)

            narrow_hi(2, "in_wg2")
            rms_pass(3)
            parts_hi(3, R_FFNG + KT)
            for a in range(A):
                eng.wait_ge(s["xn_ready"], 8)
                ins = f(g_hi[:, a, :], xn_v[:, a, :], ACT.Copy)
            ins.then_inc(s["g_hi_done"], 1)
            split_to(EX0 + AHEAD)
            eng.wait_ge(s["route_exp"], 1)
            f(REXP, REXP, ACT.Exp).then_inc(s["route_sel"], 1)

            te, ee = turns(expert_order), ends(expert_order)
            NCX, D0 = len(EXPERT_W), len(DENSE_W)
            T0 = 2 * D0

            def gathered(j):
                for b in range(2):
                    eng.wait_ge(s["gather_psum"], 2 * j + b + 1)
                    for i in range(4):
                        k = 4 * b + i
                        ins = f(hT_hi[:, k, 0:P], pB[:, 1 + b, P * i:P * (i + 1)], ACT.Copy,
                                scale=col(R_FFNG + KT + k))
                    ins.then_inc(s["xg_hi_done"], 1)

            def output_hi(j):
                eng.wait_ge(s["slot_ready"], j + 1)
                for half in range(2):
                    f(y_hi[:, 512 * half:512 * (half + 1)], pA[:, 2 + half, :], ACT.Copy,
                      scale=gslot).then_inc(s["y_hi_done"], 1)

            def job(j, first=False, last=False):
                if last:
                    cap[0] = EX0 + FFE
                if not first:
                    output_hi(j - 1)
                for t in range(FFE):
                    for c in range(NCX):
                        if t == ee["gate", c]:
                            after(EX0 + t, j)
                            eng.wait_ge(s["act_done"], D0 + NCX * j + c)
                            f(sg[:, 0, :], B0, ACT.Silu).then_inc(s["silu_done"], 1)
                        if t == te[c]:
                            after(EX0 + t, j)
                            eng.wait_ge(s["aT_psum"], T0 + NCX * j + c + 1)
                            f(aT_hi[:, c % 2, :, 0:P], bank_as(B4, 4, P), ACT.Copy).then_inc(s["aT_hi_done"], 1)
                    if t == 14:
                        split_to(EX0 + t + 1 + AHEAD, j)
                        eng.wait_ge(s["slot_psum"], j + 1)
                        if not first:
                            eng.wait_ge(s["y_lo_done"], 2 * j)
                        f(spread[:], bank_as(B7, A, P), ACT.Copy)
                        f(gslot, B7[:, S:S + 1], ACT.Copy).then_inc(s["slot_ready"], 1)
                    if t == 75 and not last:
                        after(EX0 + t, j)
                        gathered(j + 1)
                if not last:
                    after(EX0 + FFE - 1, j)
                    nxt[0] -= FFE
                else:
                    split_to(EX0 + FFE, j)
                    eng.wait_ge(s["w_used"], piece_count(EX0 + FFE - 1, j))
                    output_hi(j)

            gathered(0)
            job(0, first=True)
            middle = load_middle_jobs(eng)
            with eng.Fori(0, middle) as i:
                job(i + 1)
            job(middle + 1, last=True)

        @block.vector
        def _(eng):
            tt, ts, stt = nc.vector.tensor_tensor, nc.vector.tensor_scalar, nc.vector.scalar_tensor_tensor
            chain = [0]

            def link(ins):
                chain[0] += 1
                ins.then_inc(s["dve_chain"], 1)
                eng.wait_ge(s["dve_chain"], chain[0])

            nxt = [0]

            cap = [EX0 + FFE + AHEAD]

            def split_to(m_end, j=0):
                while nxt[0] < min(m_end, cap[0]):
                    m = nxt[0]
                    eng.wait_ge(s["w_hi_done"], piece_count(m, j))
                    tt(w_lo[:, m % PARTS, :], raw[:, m // 2 % RAW, PIECE * (m % 2):PIECE * (m % 2 + 1)],
                       w_hi[:, m % PARTS, :].bitcast(F32), ALU.subtract).then_inc(s["w_lo_done"], 1)
                    nxt[0] += 1

            def after(m, j=0):
                split_to(m + 1 + AHEAD, j)
                eng.wait_ge(s["w_used"], piece_count(m, j))

            def norm(q):
                for a in range(A):
                    eng.wait_ge(s["rms_ready"], A * q + a + 1)
                    link(nc.vector.reciprocal(RSTD[:, a:a + 1], RMS[:, a:a + 1]))
                    ts(xn_v[:, a, :], x[:, a, :], RSTD[:, a:a + 1], None, ALU.mult).then_inc(s["xn_ready"], 1)

            def parts_lo(q, g_row):
                for b in range(4):
                    eng.wait_ge(s["hT_hi_done"], 4 * q + b + 1)
                    for i in range(2):
                        k = 2 * b + i
                        ins = stt(hT_lo[:, k, :], pB[:, b, S * i:S * (i + 1)], col(g_row + k),
                                  hT_hi[:, k, :].bitcast(F32), ALU.mult, ALU.subtract)
                    ins.then_inc(s["hT_lo_done"], 1)

            def narrow_lo(n):
                eng.wait_ge(s["wg_hi_done"], n + 1)
                tt(wg_lo[:], wg_raw[:], wg_hi[:].bitcast(F32), ALU.subtract).then_inc(s["wg_lo_done"], 1)

            def narrow_rows(n):
                eng.wait_ge(s["narrow_psum"], n)
                nc.vector.tensor_copy(narrow_sb[:], B0[0:8, 0:S]).then_inc(s["narrow_rows"], 1)

            def mixer(layer):
                m0 = M0[layer]
                norm(2 * layer)
                if layer == 0:
                    narrow_lo(0)
                parts_lo(2 * layer, R_MIXG + KT * layer)
                if layer == 1:
                    narrow_lo(1)
                narrow_rows(layer + 1)
                split_to(m0 + 2)
                eng.wait_ge(s["gate_psum"], layer + 1)
                if layer == 0:
                    eng.wait_ge(s["in_bias"], 16 * 7)
                pre = PRE.rearrange("p (a g) -> p a g", a=A)
                link(tt(pre, bank_as(B1, A, 8), gbias[:, layer:layer + 1, :].broadcast_to([P, A, 8]), ALU.add))
                ip, fp = pre[:, :, 0:MH], pre[:, :, MH:]
                v8 = [t.rearrange("p (a h) -> p a h", a=A) for t in (NABS, MINF, LF, BC, RR, RMAX, MU, DEN)]
                nabs, minf, lf, bc, rr, rmax, mu, den = v8
                ts(minf, fp, 0.0, None, ALU.min)
                stt(nabs, fp, -1.0, fp, ALU.mult, ALU.min).then_inc(s["gate_pre"], 1)
                eng.wait_ge(s["soft_ready"], layer + 1)
                tt(LF, MINF, LN1, ALU.subtract).then_inc(s["lf_ready"], 1)
                split_to(m0 + 4 + AHEAD)
                if layer == 0:
                    eng.wait_ge(s["brow_psum"], 1)
                    tt(brow_sb, B6[0:AH, 0:BT], bmask_sb, ALU.add).then_inc(s["brow_ready"], 1)
                eng.wait_ge(s["cum_psum"], layer + 1)
                link(nc.vector.tensor_copy(BC, B5[:, 0:8]))
                link(tt(rr, ip, bc, ALU.subtract))
                for a in range(A):
                    for h in range(MH):
                        ins = ts(Wt[:, a, h, :], ident, RR[:, MH * a + h:MH * a + h + 1], None, ALU.mult)
                ins.then_inc(s["diag_ready"], 1)
                split_to(m0 + 6 + AHEAD)
                eng.wait_ge(s["rb_psum"], layer + 1)
                for a in range(A):
                    link(tt(Wt[:, a], bank_as(pB[:, 2 + a, :], MH, P),
                            cst[:, CAUSAL:CAUSAL + 1, :].broadcast_to([P, MH, P]), ALU.add))
                    link(nc.vector.tensor_reduce(rmax[:, a, :], Wt[:, a], AX, ALU.max))
                link(ts(MU[:, 0:MH], RMAX[:, 0:MH], 0.0, None, ALU.max))
                link(nc.vector.tensor_copy(ST0[:, 0:MH], MU[:, 0:MH]))
                tt(ST0[:, MH:], MU[:, 0:MH], BC[:, 0:MH], ALU.add).then_inc(s["mu0_ready"], 1)
                split_to(m0 + 9 + AHEAD)
                eng.wait_ge(s["mulast_psum"], layer + 1)
                link(nc.vector.tensor_copy(MLAST, B7[:, 0:8]))
                link(tt(MU[:, MH:], RMAX[:, MH:], MLAST[:, MH:], ALU.max))
                link(ts(NMU, MU, -1.0, None, ALU.mult))
                tt(EARG[:, 0:MH], MLAST[:, MH:], MU[:, MH:], ALU.subtract)
                tt(EARG[:, MH:2 * MH], RR[:, 0:MH], MLAST[:, 0:MH], ALU.subtract)
                tt(EARG[:, 2 * MH:], NMU, BC, ALU.subtract).then_inc(s["exp_args"], 1)
                split_to(m0 + 10 + AHEAD)
                eng.wait_ge(s["lin_evac"], NCH * layer + 2)
                for t in range(2 * MH):
                    if t % 2 == 1:
                        split_to(m0 + 11 + t // 2 + AHEAD)
                    for tap in range(TAPS):
                        src = conv_in[:, t, tap:tap + S]
                        wc = col(R_CONVW + (layer * TAPS + tap) * KT + t)
                        if tap == 0:
                            link(ts(qk[:, t, :], src, wc, col(R_CONVB + layer * KT + t), ALU.mult, ALU.add))
                        else:
                            ins = stt(qk[:, t, :], src, wc, qk[:, t, :], ALU.mult, ALU.add)
                            if tap < TAPS - 1:
                                link(ins)
                ins.then_inc(s["conv_ready"], 1)
                after(m0 + 18)
                for a in range(A):
                    eng.wait_ge(s["w_ready"], layer + 1)
                    eng.wait_ge(s["qk_psum"], A * layer + a + 1)
                    link(stt(Wt[:, a], bank_as(pB[:, a, :], MH, P), float(MD) ** -0.5, Wt[:, a], ALU.mult, ALU.mult))
                    nc.vector.tensor_reduce(den[:, a, :], Wt[:, a], AX, ALU.add).then_inc(s["s_ready"], 1)
                eng.wait_ge(s["kt_psum"], layer + 1)
                for h in range(MH):
                    ins = ts(kw[:, h, :], B6[:, P * h:P * (h + 1)], EARG[:, MH + h:MH + h + 1], float(MD) ** -0.5,
                             ALU.mult, ALU.mult)
                ins.then_inc(s["kw_ready"], 1)
                split_to(m0 + 25 + AHEAD)
                expnm = EARG[:, 2 * MH:].rearrange("p (a h) -> p a h", a=A)
                for a in range(A):
                    if a == 1:
                        eng.wait_ge(s["state_ready"], layer + 1)
                        link(tt(den[:, 1, :], den[:, 1, :], st_sb[:, :, MD], ALU.add))
                    link(stt(den[:, a, :], den[:, a, :], -1.0, den[:, a, :], ALU.mult, ALU.max))
                    link(tt(den[:, a, :], den[:, a, :], expnm[:, a, :], ALU.max))
                    link(nc.vector.reciprocal(den[:, a, :], den[:, a, :]))
                    eng.wait_ge(s["num_psum"], A * layer + a + 1)
                    num = bank_as(pB[:, a, :], MH, MD)
                    h4 = Wt[:, a]
                    if a == 1:
                        link(tt(h4, num, st_sb[:, :, 0:MD], ALU.add))
                        num = h4
                    link(tt(h4, num, den[:, a, :].unsqueeze(2).broadcast_to([P, MH, MD]), ALU.mult))
                    if a == 0:
                        eng.wait_ge(s["lin_evac"], NCH * layer + 4)
                    so4 = so[:, a, :].rearrange("p (h d) -> p h d", h=MH)
                    link(tt(so4, so4, h4, ALU.mult))
                    link(tt(h4, so4, so4, ALU.mult))
                    ins = nc.vector.tensor_reduce(CSS[:, MH * a:MH * (a + 1)], h4, AX, ALU.add)
                    if a == 0:
                        link(ins)
                        split_to(m0 + 26 + AHEAD)
                ins.then_inc(s["cell_ss"], 1)
                split_to(m0 + 27 + AHEAD)
                eng.wait_ge(s["cell_rms"], layer + 1)
                link(nc.vector.reciprocal(CRMS, CRMS))
                sov = so[:].rearrange("p a (h d) -> p (a h) d", h=MH)
                tt(sov, sov, CRMS.unsqueeze(2).broadcast_to([P, A * MH, MD]), ALU.mult).then_inc(s["ha_ready"], 1)
                eng.wait_ge(s["lin_evac"], NCH * layer + 6)
                qkh = aqk[:].rearrange("p w a (h d) -> p (w a h) d", h=AH)
                sq = gbv[:, 0:2 * A * AW].rearrange("p (b d) -> p b d", d=AD)
                link(tt(sq, qkh, qkh, ALU.mult))
                nc.vector.tensor_reduce(QSS, sq, AX, ALU.add).then_inc(s["qkn_ss"], 1)
                eng.wait_ge(s["qkn_rms"], layer + 1)
                link(nc.vector.reciprocal(QRMS, QRMS))
                tt(qkh, qkh, QRMS.unsqueeze(2).broadcast_to([P, 4 * AH, AD]), ALU.mult).then_inc(s["qkn_ready"], 1)
                for b in range(2):
                    eng.wait_ge(s["haT_hi_done"], 2 * layer + b + 1)
                    for i in range(2):
                        h = 2 * b + i
                        ins = stt(haT_lo[:, h, :], pB[:, 2 + b, S * i:S * (i + 1)], col(R_MNG + MH * layer + h),
                                  haT_hi[:, h, :].bitcast(F32), ALU.mult, ALU.subtract)
                    ins.then_inc(s["haT_lo_done"], 1)
                if layer == 0:
                    split_to(m0 + 29 + AHEAD)
                    eng.wait_ge(s["flip_psum"], 1)
                    nc.vector.tensor_copy(toep[:].rearrange("p h j -> p (h j)"),
                                          pB[:].rearrange("p b c -> p (b c)")).then_inc(s["toep_ready"], 1)
                split_to(m0 + 32 + AHEAD)
                for h in range(AH):
                    n = AH * layer + h
                    split_to(m0 + min(33 + max(h - 1, 0), 40) + AHEAD)
                    eng.wait_ge(s["lg_psum"], n + 1)
                    if h >= 2:
                        eng.wait_ge(s["PT_psum"], n - 1)
                    o, l = pB[:, h % 2, :], L[h % 2]
                    stt(l[:, 0:P], o[:, 0:P], float(AD) ** -0.5, toep[:, h, P:S], ALU.mult, ALU.add)
                    link(stt(l[:, P:P + S], o[:, P:P + S], float(AD) ** -0.5, toep[:, h, :], ALU.mult, ALU.add))
                    nc.vector.tensor_reduce(MX[:, 2 * h:2 * h + 1], l[:, 0:P], AX, ALU.max)
                    link(nc.vector.tensor_reduce(MX[:, 2 * h + 1:2 * h + 2], l[:, P:P + S], AX, ALU.max))
                    ts(MX[:, 2 * h:2 * h + 2], MX[:, 2 * h:2 * h + 2], -1.0, None, ALU.mult).then_inc(s["L_ready"], 1)
                    if h == 5 or h == 7:
                        q = h // 6
                        if q:
                            split_to(m0 + 41 + AHEAD)
                        eng.wait_ge(s["o_psum"], AH * layer + 4 * q + 4)
                        sums = SUMS[:, 8 * q:8 * q + 8]
                        link(nc.vector.reciprocal(sums, sums))
                        o4 = bank_as(B7, A, 4, AD)
                        for a in range(A):
                            r = sums.rearrange("p (h a) -> p a h", a=A)[:, a, :].unsqueeze(2).broadcast_to([P, 4, AD])
                            dst = ob[:, a, 4 * AD * q:4 * AD * (q + 1)].rearrange("p (h d) -> p h d", h=4)
                            ins = tt(dst, o4[:, a], r, ALU.mult)
                        ins.then_inc(s["o_evac"], 1)
                split_to(m0 + 43 + AHEAD)
                for b in range(2):
                    eng.wait_ge(s["obT_hi_done"], 2 * layer + b + 1)
                    tt(obT_lo[:, 2 * b:2 * b + 2, :], bank_as(pB[:, b, :], 2, S),
                       obT_hi[:, 2 * b:2 * b + 2, :].bitcast(F32), ALU.subtract).then_inc(s["obT_lo_done"], 1)
                after(m0 + 47)
                eng.wait_ge(s["lin_evac"], NCH * (layer + 1))
                for half in range(2):
                    for a in range(A):
                        y = ga[:, a, 512 * half:512 * (half + 1)]
                        link(tt(y, pA[:, 2 * a + half, :], y, ALU.mult))
                after(m0 + 51)
                for half in range(2):
                    for a in range(A):
                        y, z = [t[:, a, 512 * half:512 * (half + 1)] for t in (ga, gb)]
                        link(tt(z, pB[:, 2 * a + half, :], z, ALU.mult))
                        ins = tt(y, y, z, ALU.add)
                    ins.then_inc(s["y_ready"], 1)
                for b in range(4):
                    eng.wait_ge(s["yT_hi"], 4 * layer + b + 1)
                    tt(hT_lo[:, 2 * b:2 * b + 2, :], bank_as(pA[:, b, :], 2, S),
                       hT_hi[:, 2 * b:2 * b + 2, :].bitcast(F32), ALU.subtract).then_inc(s["h_parts"], 1)
                after(m0 + MIX - 1)
                add_banks(2 * layer + 1)

            def add_banks(q):
                for a in range(A):
                    for half in range(2):
                        y = x[:, a, 512 * half:512 * (half + 1)]
                        tt(y, pB[:, 2 * a + half, :], y, ALU.add).then_inc(s["x_ready"], 1)

            nc.vector.memset(vec_rows, 0.0).then_inc(s["vec_zero"], 1)
            link(nc.vector.memset(conv_in[:, :, 0:TAPS - 1], 0.0))
            mixer(0)

            norm(1)
            parts_lo(1, R_FFNG)
            ta, en = turns(dense_order), ends(dense_order)
            for t in range(FFD):
                for c, w in enumerate(DENSE_W):
                    if t == en["up", c]:
                        after(DN0 + t)
                        eng.wait_ge(s["silu_done"], c + 1)
                        if c:
                            eng.wait_ge(s["aT_psum"], 2 * c)
                        for a in range(A):
                            ins = tt(act[:, a, 0:w], pA[:, 2 + a, 0:w], sg[:, a, 0:w], ALU.mult)
                        ins.then_inc(s["act_done"], 1)
                    if t == ta[c]:
                        after(DN0 + t)
                        for b in range(2):
                            k = w // COLS + 1
                            eng.wait_ge(s["aT_hi_done"], 2 * c + b + 1)
                            tt(aT_lo[:, c % 2, k * b:k * (b + 1), :], bank_as(pA[:, 2 + b, :], k, S),
                               aT_hi[:, c % 2, k * b:k * (b + 1), :].bitcast(F32), ALU.subtract)\
                                .then_inc(s["aT_lo_done"], 1)
            after(DN0 + FFD - 1)
            add_banks(2)
            eng.wait_ge(s["x_ready"], 8)
            link(nc.vector.memset(conv_in[:, :, 0:TAPS - 1], 0.0))

            mixer(1)

            narrow_lo(2)
            norm(3)
            parts_lo(3, R_FFNG + KT)
            narrow_rows(3)
            eng.wait_ge(s["g_hi_done"], 1)
            for a in range(A):
                tt(g_lo[:, a, :], xn_v[:, a, :], g_hi[:, a, :].bitcast(F32), ALU.subtract)
            eng.wait_ge(s["logit_psum"], 1)
            iota = cst[:, IOTA, 0:NE]
            iota_b = cst[:, IOTA:IOTA + 1, 0:NE].broadcast_to([P, A, NE])
            lg = sm(8, 16).rearrange("p (a e) -> p a e", a=A)
            t1, hot1, hot2 = [sm(c, 16).rearrange("p (a e) -> p a e", a=A) for c in (24, 40, 56)]
            m1, m2, idx = sm(72, A), sm(74, A), sm(76, A)

            def wide(t):
                return t.unsqueeze(2).broadcast_to([P, A, NE])

            def top(m, hot):
                link(nc.vector.tensor_reduce(m, lg, AX, ALU.max))
                link(tt(t1, lg, wide(m), ALU.is_equal))
                link(stt(t1, t1, -8.0, iota_b, ALU.mult, ALU.add))
                link(nc.vector.tensor_reduce(idx, t1, AX, ALU.min))
                link(ts(idx, idx, 8.0, None, ALU.add))
                link(tt(hot, iota_b, wide(idx), ALU.is_equal))

            link(nc.vector.tensor_copy(lg, bank_as(B1, A, 8)))
            top(m1, hot1)
            link(stt(lg, hot1, NEG, lg, ALU.mult, ALU.add))
            top(m2, hot2)
            tt(REXP, m2, m1, ALU.subtract).then_inc(s["route_exp"], 1)
            sel = sel_v
            tt(sel, hot1, hot2, ALU.add).then_inc(s["sel_ready"], 1)

            def gate_table():
                eng.wait_ge(s["route_sel"], 1)
                link(ts(m1, REXP, 1.0, None, ALU.add))
                link(nc.vector.reciprocal(m1, m1))
                link(tt(m2, m1, REXP, ALU.mult))
                link(tt(hot1, hot1, wide(m1), ALU.mult))
                link(tt(hot2, hot2, wide(m2), ALU.mult))
                for r in range(ROUNDS):
                    link(tt(gates[:, :, NE * r:NE * (r + 1)], hot1, hot2, ALU.add))

            eng.wait_ge(s["rank_psum"], 1)
            link(nc.vector.tensor_reduce(idx[:, 0:1], B5[:, 16:24], AX, ALU.max))
            link(ts(idx[:, 0:1], idx[:, 0:1], P + 0.5, float(JOBS - NE), ALU.is_gt, ALU.mult))
            ts(middle_jobs[:], idx[:, 0:1], NE - 2.0, None, ALU.add).then_inc(s["middle_ready"], 1)
            link(ts(t1, bank_as(B5, A, 8), 1.0, None, ALU.add))
            link(tt(t1, t1, sel, ALU.mult))
            for r in range(ROUNDS):
                link(ts(keys[:, :, NE * r:NE * (r + 1)], t1, -1.0 - P * r, None, ALU.add))
            link(nc.vector.memset(jcount, 0.0))

            def choose(j, before_gates=None):
                hj = sm(104, JOBS)
                prod = sm(120, A * JOBS).rearrange("p (a e) -> p a e", a=A)
                hw = hj.unsqueeze(1).broadcast_to([P, A, JOBS])
                ch = [0]

                def lk(ins):
                    ch[0] += 1
                    ins.then_inc(s["choose_chain"], 1)
                    eng.wait_ge(s["choose_chain"], CHOOSE * j + ch[0])

                lk(ts(hj, cst[:, IOTA, 0:JOBS], jcount, None, ALU.is_equal))
                lk(ts(jcount, jcount, 1.0, None, ALU.add))
                lk(tt(prod, keys[:], hw, ALU.mult))
                lk(nc.vector.tensor_reduce(kcur, prod, AX, ALU.add))
                for a in range(A):
                    ins = ts(pick[:, a, :], cst[:, IOTA, :], kcur[:, a:a + 1], None, ALU.is_equal)
                ins.then_inc(s["pick_ready"], 1)
                if before_gates:
                    before_gates()
                lk(tt(prod, gates[:], hw, ALU.mult))
                lk(nc.vector.tensor_reduce(gcur, prod, AX, ALU.add))
                assert ch[0] == CHOOSE

            te, ee = turns(expert_order), ends(expert_order)
            NCX, D0 = len(EXPERT_W), len(DENSE_W)
            T0 = 2 * D0

            def gathered(j):
                for b in range(2):
                    eng.wait_ge(s["xg_hi_done"], 2 * j + b + 1)
                    for i in range(4):
                        k = 4 * b + i
                        ins = stt(hT_lo[:, k, 0:P], pB[:, 1 + b, P * i:P * (i + 1)], col(R_FFNG + KT + k),
                                  hT_hi[:, k, 0:P].bitcast(F32), ALU.mult, ALU.subtract)
                    ins.then_inc(s["xg_lo_done"], 1)

            def output_lo(j):
                for half in range(2):
                    cols = slice(512 * half, 512 * (half + 1))
                    eng.wait_ge(s["y_hi_done"], 2 * j + half + 1)
                    stt(y_lo[:, cols], pA[:, 2 + half, :], gslot, y_hi[:, cols].bitcast(F32),
                        ALU.mult, ALU.subtract).then_inc(s["y_lo_done"], 1)

            def add_half(j, half, last=False):
                for a in range(A):
                    eng.wait_ge(s["scatter_psum"], 4 * j + 2 * half + a + 1)
                    y = x[:, a, 512 * half:512 * (half + 1)]
                    tt(y, pA[:, a, :] if last else pB[:, 1 + a, :], y, ALU.add).then_inc(s["added"], 1)

            def job(j, first=False, last=False):
                if last:
                    cap[0] = EX0 + FFE
                if not first:
                    output_lo(j - 1)
                for t in range(FFE):
                    for c in range(NCX):
                        if t == ee["up", c]:
                            after(EX0 + t, j)
                            eng.wait_ge(s["silu_done"], D0 + NCX * j + c + 1)
                            eng.wait_ge(s["aT_psum"], T0 + NCX * j + c)
                            tt(act[:, 0, :], B1, sg[:, 0, :], ALU.mult).then_inc(s["act_done"], 1)
                        if t == te[c]:
                            after(EX0 + t, j)
                            eng.wait_ge(s["aT_hi_done"], T0 + NCX * j + c + 1)
                            tt(aT_lo[:, c % 2, :, 0:P], bank_as(B4, 4, P), aT_hi[:, c % 2, :, 0:P].bitcast(F32),
                               ALU.subtract).then_inc(s["aT_lo_done"], 1)
                    if t in (3, 10) and not first:
                        split_to(EX0 + t + 1 + AHEAD, j)
                        add_half(j - 1, t // 10)
                    if t == 20 and not last:
                        after(EX0 + t, j)
                        eng.wait_ge(s["slot_psum"], j + 1)
                        choose(j + 1)
                    if t == 75 and not last:
                        after(EX0 + t, j)
                        gathered(j + 1)
                if not last:
                    after(EX0 + FFE - 1, j)
                    nxt[0] -= FFE
                else:
                    split_to(EX0 + FFE, j)
                    output_lo(j)
                    add_half(j, 0)
                    add_half(j, 1, last=True)

            choose(0, gate_table)
            split_to(EX0 + AHEAD)
            gathered(0)
            job(0, first=True)
            middle = load_middle_jobs(eng)
            with eng.Fori(0, middle) as i:
                job(i + 1)
            job(middle + 1, last=True)


def tables():
    import numpy as np

    r = np.arange(P)
    c = np.zeros((P, 8, P), np.float32)
    c[:, IDENT] = r[:, None] == r
    c[:, TRIU] = r[:, None] <= r
    c[:, STRICT] = r[:, None] < r
    c[P - 1, LAST] = 1
    c[:, FLIP] = r[:, None] == P - 1 - r
    c[:, CAUSAL] = np.where(r[:, None] >= r, 0, NEG)
    c[:, IOTA] = r
    c[:, ONES] = 1
    buckets, exact, furthest = 32, 16, 1024
    n = (S - 1 - np.arange(BT)).clip(0)
    ratio = np.log(np.maximum(n, exact).astype(np.float32) / np.float32(exact)) / np.float32(np.log(furthest / exact))
    large = np.minimum(exact + (ratio * np.float32(buckets - exact)).astype(np.int32), buckets - 1)
    bucket = np.where(n < exact, n, large)
    past = np.arange(BT) < S
    hot = ((np.arange(buckets)[:, None] == bucket) & past).astype(np.float32)
    mask = np.broadcast_to(np.where(past, 0, NEG).astype(np.float32), (AH, BT)).copy()
    return c.reshape(P, 8 * P), hot, mask


_INS = ["x", "rel_bias", "mix_norm_g", "w_in", "conv_w", "conv_b", "igate_b", "fgate_b", "mlstm_norm_g",
        "q_norm_g", "k_norm_g", "w_branch_a", "w_branch_b", "w_out", "ffn_norm_g", "dense_w_gate", "dense_w_up",
        "dense_w_down", "router_w", "expert_w_gate", "expert_w_up", "expert_w_down"]


def kernel(**inputs):
    import numpy as np
    import concourse.bacc as bacc
    from concourse.bass_utils import run_bass_kernel_spmd as run

    nc = bacc.Bacc("TRN2", target_bir_lowering=False, num_devices=1)
    arrays = {f"{n}_dram": np.ascontiguousarray(inputs[n]) for n in _INS}
    arrays.update(zip(("consts_dram", "bucket_hot_dram", "bucket_mask_dram"), tables()))
    args = [nc.dram_tensor(n, a.shape, mybir.dt.from_np(a.dtype), kind="ExternalInput").ap()
            for n, a in arrays.items()]
    args.append(nc.dram_tensor("bias_rows_dram", (AH, BT), F32, kind="Internal").ap())
    args.append(nc.dram_tensor("out_dram", (1, S, D), F32, kind="ExternalOutput").ap())
    program(nc, *args)
    return run(nc, [arrays], core_ids=[0]).results[0]["out_dram"]
```

```python
from contextlib import ExitStack

import concourse.bass as bass
from concourse import mybir

F32 = mybir.dt.float32
F32R = mybir.dt.float32r
I32 = mybir.dt.int32
ALU = mybir.AluOpType
ACT = mybir.ActivationFunctionType
AX = mybir.AxisListType.X

P = 128
D = 1024
KT = D // P
S = 256
A = S // P
NL = 2
MH, MD = 4, 128
AH, AD = 8, 64
MW, AW = MH * MD, AH * AD
TAPS = 4
FD = 2816
NE, FE = 8, 3584
EPS = 1e-6
NEG = -1e30

UNIT, PIECE = 2048, 1024
RAW = 6
RING = 21
PARTS = 6
AHEAD = 4

COLS = 512
MIX = 60
FFD = FD // COLS * 12 + 6
FFE = FE // COLS * 12
M0 = [0, MIX + FFD]
DN0 = MIX
EX0 = 2 * MIX + FFD
assert EX0 % PARTS == 0 and FFE % PARTS == 0 and FFE % RING == 0 and FD % COLS == 256

ROUNDS = 2
JOBS = ROUNDS * NE
CHOOSE = 6

Q0, K0, V0, O0, G0 = 0, MW, 2 * MW, 3 * MW, 4 * MW
AQ0 = G0 + 2 * MH
GA0 = AQ0 + 3 * AW
CHUNK_COLS = [Q0, K0, V0, O0, AQ0, AQ0 + AW, AQ0 + 2 * AW] + [GA0 + COLS * i for i in range(4)]
NCH = len(CHUNK_COLS)

IDENT, TRIU, STRICT, LAST, FLIP, CAUSAL, IOTA, ONES = range(8)
R_MIXG, R_FFNG, R_CONVW, R_CONVB, R_MNG, R_QG, R_KG = 0, 16, 32, 96, 112, 120, 122
NVEC = 124
BT = 384


def ffn_order(widths):
    order, at = [], 0
    n = len(widths)
    for c in range(n + 1):
        for kind, cc in (("gate", c), ("up", c), ("down", c - 1)):
            if 0 <= cc < n and (kind == "down" or c < n):
                pieces = 4 * widths[cc] // COLS
                order.append((kind, cc, at, pieces))
                at += pieces
    return order, at


DENSE_W = [COLS] * (FD // COLS) + [FD % COLS]
EXPERT_W = [COLS] * (FE // COLS)


def program(nc, x_in, rel_bias, mix_norm_g, w_in, conv_w, conv_b, igate_b, fgate_b, mlstm_norm_g,
            q_norm_g, k_norm_g, w_branch_a, w_branch_b, w_out, ffn_norm_g, dense_gate, dense_up, dense_down,
            router_w, expert_gate, expert_up, expert_down, consts, bucket_hot, bucket_mask, bias_rows, out):
    with ExitStack() as ctx:
        def sb(name, shape, dt=F32):
            return ctx.enter_context(nc.sbuf_tensor(name, shape, dt))

        def sem(name):
            return ctx.enter_context(nc.semaphore(name))

        raw = sb("raw", [P, RAW, UNIT])
        w_hi = sb("w_hi", [P, PARTS, PIECE], F32R)
        w_lo = sb("w_lo", [P, PARTS, PIECE], F32R)
        x = sb("x", [P, A, D])
        hT_hi = sb("hT_hi", [P, KT, S], F32R)
        hT_lo = sb("hT_lo", [P, KT, S], F32R)
        g_hi = sb("g_hi", [P, A, D], F32R)
        g_lo = sb("g_lo", [P, A, D], F32R)
        cst = sb("cst", [P, 8, P])
        vec = sb("vec", [P, P])
        toep = sb("toep", [P, AH, S])
        gbias = sb("gbias", [P, NL, 2 * MH])
        small = sb("small", [P, 256])
        rt = sb("rt", [P, 32])
        middle_jobs = sb("middle_jobs", [P, 1], I32)
        narrow_sb = sb("narrow_sb", [8, S])
        eps = sb("eps", [P, 1])
        one = sb("one", [P, 1])
        wg_raw = sb("wg_raw", [P, KT, 8])
        wg_hi = sb("wg_hi", [P, KT, 8], F32R)
        wg_lo = sb("wg_lo", [P, KT, 8], F32R)

        mix = ExitStack()

        def mb(name, shape, dt=F32):
            return mix.enter_context(nc.sbuf_tensor(name, shape, dt))

        conv_in = mb("conv_in", [P, 2 * MH, TAPS - 1 + S])
        qk = mb("qk", [P, 2 * MH, S])
        v = mb("v", [P, A, MW])
        so = mb("so", [P, A, MW])
        aqk = mb("aqk", [P, 2, A, AW])
        av = mb("av", [P, A, AW])
        ga = mb("ga", [P, A, D])
        gb = mb("gb", [P, A, D])
        mix.close()
        ffn = ExitStack()

        def fb(name, shape, dt=F32):
            return ffn.enter_context(nc.sbuf_tensor(name, shape, dt))

        aT_hi = fb("aT_hi", [P, 2, 4, S], F32R)
        aT_lo = fb("aT_lo", [P, 2, 4, S], F32R)
        sg = fb("sg", [P, A, COLS])
        act = fb("act", [P, A, COLS])
        ffn.close()
        moe = ExitStack()

        def eb(name, shape, dt=F32):
            return moe.enter_context(nc.sbuf_tensor(name, shape, dt))

        more = eb("more", [P, RING - 2 * RAW - 2, PIECE])
        ex_hi = eb("ex_hi", [P, 2, 4, P], F32R)
        ex_lo = eb("ex_lo", [P, 2, 4, P], F32R)
        ex_sg = eb("ex_sg", [P, COLS])
        ex_act = eb("ex_act", [P, COLS])
        pick = eb("pick", [P, A, P], F32R)
        spread = eb("spread", [P, A, P], F32R)
        keys = eb("keys", [P, A, JOBS])
        gates = eb("gates", [P, A, JOBS])
        y_hi = eb("y_hi", [P, D], F32R)
        y_lo = eb("y_lo", [P, D], F32R)
        moe.close()

        xn_v = gb[:]
        civ = conv_in[:].rearrange("p a b -> p (a b)")
        n = MH * (MD + 1)
        kw = civ[:, 0:MH * MD].rearrange("p (h d) -> p h d", h=MH)
        caug, st_sb = [civ[:, MH * MD + n * i:MH * MD + n * (i + 1)].rearrange("p (h d) -> p h d", h=MH)
                       for i in range(2)]
        qaT = civ[:, 0:4 * S].rearrange("p (a b) -> p a b", a=4)
        kaT = civ[:, 4 * S:8 * S].rearrange("p (a b) -> p a b", a=4)
        aqv = aqk[:].rearrange("p a b c -> p (a b c)")
        hot_sb, bmask_sb, brow_sb = aqv[0:32, 0:BT], aqv[0:AH, BT:2 * BT], aqv[0:AH, 2 * BT:3 * BT]
        rb_sb, vec_rows = aqv[0:32, 3 * BT:3 * BT + AH], aqv[:, 10 * P:11 * P]
        L = [aqv[:, 384 * i:384 * (i + 1)] for i in range(2)]
        PT = [aqv[:, 768 + 384 * i:768 + 384 * (i + 1)] for i in range(2)]
        gbv = gb[:].rearrange("p a b -> p (a b)")
        Wt = gbv[:, 0:A * MH * P].rearrange("p (a h s) -> p a h s", a=A, h=MH)
        sq_v = ga[:].rearrange("p a b -> p (a b)")[:, 0:2 * A * AW]
        sT = gbv[:, A * MH * P:2 * A * MH * P].rearrange("p (a h s) -> p a h s", a=A, h=MH)
        ob = v
        haT_hi, haT_lo = [t[:, 0, :].rearrange("p (h s) -> p h s", h=MH) for t in (g_hi, g_lo)]
        obT_hi, obT_lo = [t[:, 1, :].rearrange("p (h s) -> p h s", h=4) for t in (g_hi, g_lo)]

        pA = ctx.enter_context(nc.psum_tensor("pA", [P, 4, 512], F32))
        pB = ctx.enter_context(nc.psum_tensor("pB", [P, 4, 512], F32))

        def block_of(i):
            return cst[:, i, :]

        ident = block_of(IDENT)

        def col(c, n=1):
            return vec[:, c:c + n]

        def bank_as(bank, *dims):
            n = 1
            for d in dims:
                n *= d
            names = "abc"[:len(dims)]
            kw_ = {c: d for c, d in zip(names, dims)}
            return bank[:, 0:n].rearrange(f"p ({' '.join(names)}) -> p {' '.join(names)}", **kw_)

        B0, B1, B2, B3 = [pA[:, i, :] for i in range(4)]
        B4, B5, B6, B7 = [pB[:, i, :] for i in range(4)]

        w_loaded = [sem(f"w_loaded{r}") for r in range(RAW)]
        e_loaded = [sem(f"e_loaded{r}") for r in range(RING)]
        names = ["w_hi_done", "w_lo_done", "w_used",
                 "in_x0", "in_x1", "in_cst", "in_vec", "in_bias", "in_wg0", "in_wg1", "in_wg2", "stored", "brow_stored",
                 "toep_loaded", "act_chain", "dve_chain",
                 "vec_zero", "vec_psum", "vec_ready", "brow_psum", "brow_ready", "flip_psum", "pads_ready",
                 "rms_ready", "xn_ready", "xT_psum", "hT_hi_done", "hT_lo_done", "wg_hi_done", "wg_lo_done",
                 "x_ready", "lin_evac", "gate_psum", "gate_pre", "soft_ready", "lf_ready", "cum_psum",
                 "diag_ready", "rb_psum", "mu0_ready", "mulast_psum", "exp_args", "w_ready", "conv_ready",
                 "qk_ready", "qk_psum", "s_ready", "sT_psum", "sT_ready", "kt_psum", "kw_ready", "c_psum",
                 "c_ready", "state_psum", "state_ready", "num_psum", "cell_ss", "cell_rms", "ha_ready",
                 "haT_psum", "haT_hi_done", "haT_lo_done", "qkn_sq", "qkn_ss", "qkn_rms", "qkn_ready", "qaT_psum",
                 "qaT_ready", "lg_psum", "L_ready", "P_ready", "PT_psum", "PT_ready", "o_psum", "o_evac",
                 "obT_hi_done", "obT_psum", "obT_lo_done", "y_ready", "yT_psum",
                 "silu_done", "act_done", "aT_psum", "aT_hi_done", "aT_lo_done", "h_parts",
                 "logit_psum", "route_exp", "route_sel", "sel_ready", "rank_psum", "pick_ready", "slot_psum",
                 "slot_ready", "gather_psum", "xg_hi_done", "xg_lo_done", "y_hi_done", "y_lo_done",
                 "scatter_psum", "added", "yT_hi", "g_hi_done", "choose_chain", "middle_ready", "toep_ready",
                 "narrow_psum", "narrow_rows"]
        s = {n: sem(n) for n in names}

        block = ctx.enter_context(nc.Block())

        def raw_slot(m):
            if m < EX0:
                return raw[:, (m - EX0) // 2 % RAW, PIECE * (m % 2):PIECE * (m % 2 + 1)]
            r = (m - EX0) % RING
            if r < 2 * RAW:
                return raw[:, r // 2, PIECE * (r % 2):PIECE * (r % 2 + 1)]
            if r < RING - 2:
                return more[:, r - 2 * RAW, :]
            return toep[:].rearrange("p h j -> p (h j)")[:, PIECE * (r - RING + 2):PIECE * (r - RING + 3)]

        def wait_loaded(eng, m, j):
            if m < EX0:
                eng.wait_ge(w_loaded[m // 2 % RAW], 16 * (m // 2 // RAW + 1))
            else:
                e = m - EX0
                eng.wait_ge(e_loaded[e % RING], 16 * (e // RING + 1) + 16 * (FFE // RING) * j)

        def piece_count(m, j):
            return m + 1 + FFE * j

        dense_order, n = ffn_order(DENSE_W)
        assert n == FFD
        expert_order, n = ffn_order(EXPERT_W)
        assert n == FFE

        def ends(order):
            return {(k, c): at + n - 1 for k, c, at, n in order}

        def turns(order):
            at = {}
            for i, (kind, c, start, n) in enumerate(order):
                if kind == "gate" and c > 0:
                    at[c - 1] = start + n // 2 - 1
            (kind, c, start, n) = order[-2]
            at[c + 1] = start + n // 2 - 1
            return at

        def load_middle_jobs(eng):
            eng.wait_ge(s["middle_ready"], 1)
            return eng.value_load(middle_jobs[0:1, 0:1], min_val=NE - 2, max_val=JOBS - 2)

        @block.sync
        def _(sp):
            for a in range(A):
                sp.dma_start(x[:, a, :], x_in[0, P * a:P * (a + 1), :]).then_inc(s[f"in_x{a}"], 16)
            sp.dma_start(cst[:], consts.rearrange("p (b c) -> p b c", b=8)).then_inc(s["in_cst"], 16)
            rows = [(R_MIXG, mix_norm_g.rearrange("l (k p) -> (l k) p", p=P)),
                    (R_FFNG, ffn_norm_g.rearrange("l (k p) -> (l k) p", p=P)),
                    (R_CONVW, conv_w.rearrange("l t (k p) -> (l t k) p", p=P)),
                    (R_CONVB, conv_b.rearrange("l (k p) -> (l k) p", p=P)),
                    (R_MNG, mlstm_norm_g.rearrange("l (k p) -> (l k) p", p=P))]
            sp.wait_ge(s["vec_zero"], 1)
            for r, src in rows:
                sp.dma_start(vec_rows[r:r + src.shape[0], :], src).then_inc(s["in_vec"], 16)

            sp.wait_ge(s["in_vec"], 16 * 9)
            sp.wait_ge(s["in_wg0"], 16)

            def unit_slot(u):
                return raw[:, (u - EX0 // 2) % RAW, :]

            def load(u, src, shape):
                if u >= RAW:
                    sp.wait_ge(s["w_lo_done"], 2 * (u - RAW) + 2)
                dst = unit_slot(u).rearrange("p (k n) -> p k n", k=shape)
                sp.dma_start(dst, src).then_inc(w_loaded[u % RAW], 16)

            def k_major(w, u, c0, cols):
                wv = w.rearrange("(k p) n -> p k n", p=P)
                kn = UNIT // cols
                for i in range(w.shape[0] // P // kn):
                    load(u + i, wv[:, kn * i:kn * (i + 1), c0:c0 + cols], kn)

            def n_major(w, u, k0, kn):
                wv = w.rearrange("(k p) n -> p k n", p=P)
                for i in range(kn // 2):
                    load(u + i, wv[:, k0 + 2 * i:k0 + 2 * i + 2, :], 2)

            def halved(w, u, k0):
                wv = w.rearrange("(k p) (h n) -> p h k n", p=P, h=2)
                sp.wait_ge(s["w_lo_done"], 2 * (u - RAW) + 2)
                sp.dma_start(unit_slot(u).rearrange("p (h k n) -> p h k n", h=2, k=2),
                             wv[:, :, k0:k0 + 2, :]).then_inc(w_loaded[u % RAW], 16)

            def dense():
                for kind, c, at, n in dense_order:
                    u = (DN0 + at) // 2
                    if kind == "down" and DENSE_W[c] == 2 * P:
                        halved(dense_down[0], u, 4 * c)
                    elif kind == "down":
                        n_major(dense_down[0], u, 4 * c, 4)
                    else:
                        k_major((dense_gate if kind == "gate" else dense_up)[0], u, COLS * c, DENSE_W[c])

            def expert(e, j, first=False):
                gate, up, down = [w[0][bass.ds(e, 1)].rearrange("e (k p) n -> p (e k) n", p=P)
                                  for w in (expert_gate, expert_up, expert_down)]
                for kind, c, at, n in expert_order:
                    for q in range(n):
                        r = at + q
                        if kind == "down":
                            src = down[:, 4 * c + q:4 * c + q + 1, :]
                        else:
                            src = (gate if kind == "gate" else up)[:, 2 * q:2 * q + 2, COLS * c:COLS * (c + 1)]
                        if first and r < 2 * RAW:
                            sp.wait_ge(s["w_lo_done"], EX0 + r - 2 * RAW + 1)
                        elif first and r < RING:
                            sp.wait_ge(s["obT_lo_done"], 2 * NL)
                        else:
                            sp.wait_ge(s["w_lo_done"], EX0 + r - RING + 1 + FFE * j)
                        dst = raw_slot(EX0 + r)
                        sp.dma_start(dst.rearrange("p (k n) -> p k n", k=1 if kind == "down" else 2),
                                     src).then_inc(e_loaded[r % RING], 16)

            for layer in range(NL):
                for i, c0 in enumerate(CHUNK_COLS):
                    k_major(w_in[layer], (M0[layer] + 4 * i) // 2, c0, COLS)
                u = (M0[layer] + 4 * NCH) // 2
                for half in range(2):
                    k_major(w_branch_a[layer], u + half, COLS * half, COLS)
                for half in range(2):
                    k_major(w_branch_b[layer], u + 2 + half, COLS * half, COLS)
                for half in range(2):
                    k_major(w_out[layer], u + 4 + 2 * half, COLS * half, COLS)
                if layer == 0:
                    dense()

            expert(0, 0, first=True)
            with sp.Fori(1, NE) as e:
                expert(e, e)
            middle = load_middle_jobs(sp)
            with sp.If(middle > NE):
                with sp.Fori(0, NE) as e:
                    expert(e, e + NE)
            for half in range(2):
                for a in range(A):
                    sp.wait_ge(s["added"], 4 * middle + 5 + 2 * half + a)
                    cols = slice(512 * half, 512 * (half + 1))
                    sp.dma_start(out[0, P * a:P * (a + 1), cols], x[:, a, cols]).then_inc(s["stored"], 16)
            sp.wait_ge(s["stored"], 64)

        @block.gpsimd
        def _(g):
            nc.gpsimd.memset(eps[:], EPS).then_inc(s["pads_ready"], 1)
            nc.gpsimd.memset(one[:], 1.0).then_inc(s["pads_ready"], 1)
            wif = [w_in[layer][:, G0:G0 + 8].rearrange("(k p) n -> p k n", p=P) for layer in range(NL)]
            for layer in range(NL):
                g.dma_start(gbias[:, layer, 0:MH], igate_b[layer].partition_broadcast(P)).then_inc(s["in_bias"], 16)
                g.dma_start(gbias[:, layer, MH:], fgate_b[layer].partition_broadcast(P)).then_inc(s["in_bias"], 16)
            g.dma_start(rb_sb, rel_bias).then_inc(s["in_bias"], 16)
            g.dma_start(hot_sb, bucket_hot).then_inc(s["in_bias"], 16)
            g.dma_start(bmask_sb, bucket_mask).then_inc(s["in_bias"], 16)
            g.wait_ge(s["brow_ready"], 1)
            g.dma_start(bias_rows, brow_sb).then_inc(s["brow_stored"], 16)
            g.wait_ge(s["brow_stored"], 16)
            skew = bass.AP(bias_rows.tensor, 0, [[1, P], [BT, AH], [1, S]])
            g.dma_start(toep[:], skew).then_inc(s["toep_loaded"], 16)
            g.wait_ge(s["wg_lo_done"], 1)
            g.dma_start(wg_raw[:], wif[1]).then_inc(s["in_wg1"], 16)
            g.wait_ge(s["wg_lo_done"], 2)
            g.dma_start(wg_raw[:], router_w[0].rearrange("(k p) n -> p k n", p=P)).then_inc(s["in_wg2"], 16)

        REXP, jcount, kcur, gcur, gslot = rt[:, 0:A], rt[:, 2:3], rt[:, 4:4 + A], rt[:, 6:6 + A], rt[:, 8:9]
        sel_v = rt[:, 16:32].rearrange("p (a e) -> p a e", a=A)

        def sm(c, n):
            return small[:, c:c + n]

        SS, RSTD, RMS, SS0 = sm(0, A), sm(2, A), sm(4, A), sm(6, A)
        PRE = sm(8, 16)
        LF = sm(24, 8)
        NABS, LN1, MINF = sm(32, 8), sm(40, 8), sm(48, 8)
        BC, RR, RMAX = sm(56, 8), sm(64, 8), sm(72, 8)
        MU, ST0, MLAST = sm(80, 8), sm(88, 8), sm(96, 8)
        NMU, EARG, DEN = sm(104, 8), sm(112, 16), sm(128, 8)
        CSS, CRMS = sm(136, 8), sm(144, 8)
        QSS, QRMS = sm(152, 32), sm(184, 32)
        MX, SUMS = sm(216, 16), sm(232, 16)

        @block.tensor
        def _(pe):
            mm = nc.tensor.matmul

            def piece(m, work, j=0):
                pe.wait_ge(s["w_lo_done"], piece_count(m, j))
                hi, lo = w_hi[:, m % PARTS, :], w_lo[:, m % PARTS, :]
                for o, (lh, ll), cols, first, swap in work:
                    for n, (l, r) in enumerate(((lh, hi), (lh, lo), (ll, hi))):
                        r = r[:, cols[0]:cols[1]]
                        ins = mm(o, r if swap else l, l if swap else r, start=first and n == 0, stop=True,
                                 skip_group_check=True)
                ins.then_inc(s["w_used"], 1)

            def left(hi, lo, k, a, n=P):
                return hi[:, k, a * n:(a + 1) * n], lo[:, k, a * n:(a + 1) * n]

            def chunk_piece(m, q, cols, banks, hi, lo, tiles, j=0):
                kn = PIECE // cols
                piece(m, [(banks[a][:, 0:cols], left(hi, lo, kn * q + i, a), (cols * i, cols * (i + 1)),
                           q == 0 and i == 0, False) for i in range(kn) for a in range(tiles)], j)

            def row_piece(m, k, opens, banks, hi, lo, tiles, j=0):
                piece(m, [(banks[a][n], left(hi, lo, k, a), (512 * n, 512 * (n + 1)), opens, False)
                          for a in range(tiles) for n in range(2)], j)

            def turn(o, src, first=True):
                return mm(o, src, ident, is_transpose=True, start=first, stop=True, skip_group_check=True)

            pe.wait_ge(s["in_cst"], 16)
            pe.wait_ge(s["in_vec"], 16 * 9)
            turn(B4[:, 0:P], vec_rows).then_inc(s["vec_psum"], 1)

            def normed_turns(q):
                if q == 0:
                    pe.wait_ge(s["vec_ready"], 1)
                for a in range(A):
                    pe.wait_ge(s["xn_ready"], A * q + a + 1)
                    for b in range(4):
                        for i in range(2):
                            k = 2 * b + i
                            ins = turn(pB[:, b, S * i + P * a:S * i + P * (a + 1)],
                                       xn_v[:, a, P * k:P * (k + 1)], i == 0 and a == 0)
                        if a == A - 1:
                            ins.then_inc(s["xT_psum"], 1)

            def narrow(q, wq):
                pe.wait_ge(s["wg_lo_done"], wq)
                for k in range(KT):
                    pe.wait_ge(s["hT_lo_done"], 4 * q + k // 2 + 1)
                    for n, (l, r) in enumerate(((wg_hi, hT_hi), (wg_hi, hT_lo), (wg_lo, hT_hi))):
                        ins = mm(B2[0:8, 0:S], l[:, k, :], r[:, k, :], start=(k == 0 and n == 0), stop=True,
                                 skip_group_check=True)
                ins.then_inc(s["narrow_psum"], 1)

            def narrow_turns(wq):
                pe.wait_ge(s["narrow_rows"], wq)
                for a in range(A):
                    ins = mm(B3[:, 8 * a:8 * a + 8], narrow_sb[:, P * a:P * (a + 1)], ident[0:8, 0:8],
                             is_transpose=True, start=(a == 0), stop=True, skip_group_check=True)
                return ins

            def halves(p4, half):
                return [p4[:, 2 * (1 - half) + a, :] for a in range(A)]

            def mixer(layer):
                m0 = M0[layer]
                normed_turns(2 * layer)
                narrow(2 * layer, layer + 1)

                def chunks(a, b):
                    for t in range(a, b):
                        i, q = t // 4, t % 4
                        banks = [pA[:, 2 * (i % 2) + n, :] for n in range(2)]
                        if q == 0 and i >= 2:
                            pe.wait_ge(s["lin_evac"], NCH * layer + i - 1)
                        if t == 4:
                            pe.wait_ge(s["gate_pre"], layer + 1)
                        if i < 2:
                            piece(m0 + t, [(banks[f // 2][:, S * (f % 2):S * (f % 2 + 1)],
                                            (hT_hi[:, 2 * q + k, :], hT_lo[:, 2 * q + k, :]),
                                            (COLS * k + P * f, COLS * k + P * (f + 1)),
                                            q == 0 and k == 0 and f % 2 == 0, True)
                                           for k in range(2) for f in range(4)])
                        else:
                            chunk_piece(m0 + t, q, COLS, banks, hT_hi, hT_lo, A)

                chunks(0, 1)
                narrow_turns(layer + 1).then_inc(s["gate_psum"], 1)
                chunks(1, 4)
                if layer == 0:
                    pe.wait_ge(s["in_bias"], 16 * 7)
                    mm(B6[0:AH, 0:BT], rb_sb, hot_sb, start=True, stop=True).then_inc(s["brow_psum"], 1)
                pe.wait_ge(s["lf_ready"], layer + 1)
                mm(B5[:, 0:8], block_of(TRIU), LF, start=True, stop=True).then_inc(s["cum_psum"], 1)
                chunks(4, 6)
                pe.wait_ge(s["diag_ready"], layer + 1)
                if layer == 0:
                    pe.wait_ge(s["brow_ready"], 1)
                for a in range(A):
                    ins = mm(pB[:, 2 + a, :], block_of(ONES), Wt[:, a].rearrange("p h s -> p (h s)"),
                             start=True, stop=True)
                ins.then_inc(s["rb_psum"], 1)
                chunks(6, 9)
                pe.wait_ge(s["mu0_ready"], layer + 1)
                mm(B7[:, 0:8], block_of(LAST), ST0, start=True, stop=True).then_inc(s["mulast_psum"], 1)
                chunks(9, 19)
                pe.wait_ge(s["qk_ready"], layer + 1)
                for a in range(A):
                    for h in range(MH):
                        tok = slice(P * a, P * (a + 1))
                        ins = mm(pB[:, a, P * h:P * (h + 1)], qk[:, h, tok], qk[:, MH + h, tok],
                                 start=(h == 0), stop=True, skip_group_check=True)
                    ins.then_inc(s["qk_psum"], 1)
                for h in range(MH):
                    ins = turn(B6[:, P * h:P * (h + 1)], qk[:, MH + h, 0:P], h == 0)
                ins.then_inc(s["kt_psum"], 1)
                chunks(19, 22)
                for a in range(A):
                    pe.wait_ge(s["s_ready"], A * layer + a + 1)
                    for h in range(MH):
                        ins = turn(pB[:, a, P * h:P * (h + 1)], Wt[:, a, h, :], h == 0)
                    ins.then_inc(s["sT_psum"], 1)
                chunks(22, 24)
                pe.wait_ge(s["kw_ready"], layer + 1)
                for h in range(MH):
                    mm(B6[:, P * h:P * (h + 1)], kw[:, h, :], v[:, 0, MD * h:MD * (h + 1)], start=(h == 0), stop=True,
                       skip_group_check=True)
                for h in range(MH):
                    ins = mm(B7[:, h:h + 1], kw[:, h, :], one_col, start=(h == 0), stop=True, skip_group_check=True)
                ins.then_inc(s["c_psum"], 1)
                chunks(24, 25)
                for a in range(A):
                    pe.wait_ge(s["sT_ready"], A * layer + a + 1)
                    for h in range(MH):
                        ins = mm(pB[:, a, MD * h:MD * (h + 1)], sT[:, a, h, :], v[:, a, MD * h:MD * (h + 1)],
                                 start=(h == 0), stop=True, skip_group_check=True)
                    ins.then_inc(s["num_psum"], 1)
                pe.wait_ge(s["c_ready"], layer + 1)
                for h in range(MH):
                    o = pB[:, 2 + h // 2, (MD + 1) * (h % 2):(MD + 1) * (h % 2 + 1)]
                    ins = mm(o, qk[:, h, P:S], caug[:, h, :], start=(h % 2 == 0), stop=True, skip_group_check=True)
                ins.then_inc(s["state_psum"], 1)
                chunks(25, 30)
                pe.wait_ge(s["ha_ready"], layer + 1)
                for b in range(2):
                    for i in range(2):
                        for a in range(A):
                            h = 2 * b + i
                            ins = turn(pB[:, 2 + b, S * i + P * a:S * i + P * (a + 1)], so[:, a, MD * h:MD * (h + 1)],
                                       i == 0 and a == 0)
                    ins.then_inc(s["haT_psum"], 1)
                chunks(30, 31)
                if layer == 0:
                    pe.wait_ge(s["toep_loaded"], 16)
                    pe.wait_ge(s["haT_lo_done"], 2)
                    tv = toep[:].rearrange("p h j -> p (h j)")
                    for n in range(4):
                        ins = mm(pB[:, n, :], block_of(FLIP), tv[:, 512 * n:512 * (n + 1)], start=True, stop=True)
                    ins.then_inc(s["flip_psum"], 1)
                chunks(31, 32)
                if layer == 0:
                    pe.wait_ge(s["toep_ready"], 1)
                pe.wait_ge(s["qkn_ready"], layer + 1)
                pe.wait_ge(s["haT_lo_done"], 2 * layer + 2)
                for w in range(2):
                    for t in range(4):
                        for a in range(A):
                            ins = turn(pB[:, 2 * w + t // 2, S * (t % 2) + P * a:S * (t % 2) + P * (a + 1)],
                                       aqk[:, w, a, P * t:P * (t + 1)], t % 2 == 0 and a == 0)
                    ins.then_inc(s["qaT_psum"], 1)
                chunks(32, 33)

                def logits(h):
                    n = AH * layer + h
                    if h == 0:
                        pe.wait_ge(s["qaT_ready"], 2 * layer + 2)
                    if h >= 2:
                        pe.wait_ge(s["L_ready"], n - 1)
                    lanes = slice(AD * (h % 2), AD * (h % 2 + 1))
                    o = pB[:, h % 2, :]
                    mm(o[:, 0:P], qaT[lanes, h // 2, 0:P], kaT[lanes, h // 2, 0:P], start=True, stop=True,
                       skip_group_check=True)
                    mm(o[:, P:P + S], qaT[lanes, h // 2, P:S], kaT[lanes, h // 2, :], start=False, stop=True,
                       skip_group_check=True).then_inc(s["lg_psum"], 1)

                def turn_probs(h):
                    n = AH * layer + h
                    pe.wait_ge(s["P_ready"], n + 1)
                    if n >= 1:
                        pe.wait_ge(s["PT_ready"], n)
                    for b in range(3):
                        ins = turn(B6[:, P * b:P * (b + 1)], L[h % 2][:, P * b:P * (b + 1)], b == 0)
                    ins.then_inc(s["PT_psum"], 1)

                def weigh(h):
                    n = AH * layer + h
                    pe.wait_ge(s["PT_ready"], n + 1)
                    if h == 4:
                        pe.wait_ge(s["o_evac"], 2 * layer + 1)
                    pt = PT[h % 2]
                    o = bank_as(B7, A, 4, AD)
                    vh = slice(AD * h, AD * (h + 1))
                    mm(o[:, 0, h % 4, :], pt[:, 0:P], av[:, 0, vh], start=(h % 4 == 0), stop=True, skip_group_check=True)
                    mm(o[:, 1, h % 4, :], pt[:, P:2 * P], av[:, 0, vh], start=False, stop=True, skip_group_check=True)
                    mm(o[:, 1, h % 4, :], pt[:, 2 * P:3 * P], av[:, 1, vh], start=False, stop=True,
                       skip_group_check=True).then_inc(s["o_psum"], 1)

                logits(0)
                logits(1)
                chunks(33, 34)
                for h in range(AH):
                    turn_probs(h)
                    chunks(34 + h, 35 + h)
                    if h + 2 < AH:
                        logits(h + 2)
                    weigh(h)
                chunks(42, 43)
                pe.wait_ge(s["o_evac"], 2 * layer + 2)
                for b in range(2):
                    for i in range(2):
                        for a in range(A):
                            t = 2 * b + i
                            ins = turn(pB[:, b, S * i + P * a:S * i + P * (a + 1)], ob[:, a, P * t:P * (t + 1)],
                                       i == 0 and a == 0)
                    ins.then_inc(s["obT_psum"], 1)
                chunks(43, 44)
                t = 44
                for n, (hi, lo, p4, done) in enumerate(((haT_hi, haT_lo, pA, "haT_lo_done"),
                                                        (obT_hi, obT_lo, pB, "obT_lo_done"))):
                    pe.wait_ge(s[done], 2 * layer + 2)
                    for half in range(2):
                        if n == 0:
                            pe.wait_ge(s["lin_evac"], NCH * layer + NCH - 1 + half)
                        for q in range(2):
                            chunk_piece(m0 + t, q, COLS, halves(p4, half), hi, lo, A)
                            t += 1

                def turn_y(half):
                    pe.wait_ge(s["y_ready"], 2 * layer + half + 1)
                    for b in range(2):
                        for i in range(2):
                            for a in range(A):
                                k = 4 * half + 2 * b + i
                                ins = turn(pA[:, 2 * half + b, S * i + P * a:S * i + P * (a + 1)],
                                           ga[:, a, P * k:P * (k + 1)], i == 0 and a == 0)
                        ins.then_inc(s["yT_psum"], 1)

                turn_y(0)
                for half in range(2):
                    for q in range(4):
                        if half == 0 and q == 2:
                            turn_y(1)
                        if half == 0:
                            pe.wait_ge(s["h_parts"], 4 * layer + q + 1)
                        chunk_piece(m0 + t, q, COLS, halves(pB, half), hT_hi, hT_lo, A)
                        t += 1

            one_col = one[:]

            mixer(0)

            normed_turns(1)
            ta = turns(dense_order)
            for kind, c, at, n in dense_order:
                if kind == "gate" and c:
                    pe.wait_ge(s["silu_done"], c)
                if kind == "up" and c:
                    pe.wait_ge(s["act_done"], c)
                    pe.wait_ge(s["aT_lo_done"], 2 * c)
                if kind == "down":
                    pe.wait_ge(s["aT_lo_done"], 2 * c + 2)
                for q in range(n):
                    m = DN0 + at + q
                    if kind == "down" and c == len(DENSE_W) - 1:
                        piece(m, [(halves(pB, q)[a], left(aT_hi[:, c % 2], aT_lo[:, c % 2], i, a),
                                   (COLS * i, COLS * (i + 1)), False, False) for i in range(2) for a in range(A)])
                    elif kind == "down":
                        row_piece(m, q, c == 0 and q == 0, [[halves(pB, h)[a] for h in range(2)] for a in range(A)],
                                  aT_hi[:, c % 2], aT_lo[:, c % 2], A)
                    else:
                        if kind == "gate" and c == 0:
                            pe.wait_ge(s["hT_lo_done"], 4 + q + 1)
                        banks = [pA[:, (0 if kind == "gate" else 2) + a, :] for a in range(A)]
                        chunk_piece(m, q, DENSE_W[c], banks, hT_hi, hT_lo, A)
                    for cc, pos in ta.items():
                        if pos == at + q:
                            pe.wait_ge(s["act_done"], cc + 1)
                            for b in range(2):
                                for i in range(2 if DENSE_W[cc] == COLS else 1):
                                    for a in range(A):
                                        k = (2 * b + i) if DENSE_W[cc] == COLS else b
                                        ins = turn(pA[:, 2 + b, S * i + P * a:S * i + P * (a + 1)],
                                                   act[:, a, P * k:P * (k + 1)], i == 0 and a == 0)
                                ins.then_inc(s["aT_psum"], 1)

            mixer(1)

            normed_turns(3)
            narrow(3, 3)
            narrow_turns(3).then_inc(s["logit_psum"], 1)
            pe.wait_ge(s["hT_lo_done"], 16)
            pe.wait_ge(s["sel_ready"], 1)
            sel = sel_v
            mm(B5[:, 0:8], block_of(STRICT), sel[:, 0, :], start=True, stop=True, skip_group_check=True)
            mm(B5[:, 8:16], block_of(ONES), sel[:, 0, :], start=False, stop=True, skip_group_check=True)
            mm(B5[:, 8:16], block_of(STRICT), sel[:, 1, :], start=False, stop=True, skip_group_check=True)
            for a in range(A):
                ins = mm(B5[:, 16:24], block_of(ONES), sel[:, a, :], start=False, stop=True, skip_group_check=True)
            ins.then_inc(s["rank_psum"], 1)

            te = turns(expert_order)
            NCX = len(EXPERT_W)
            D0 = len(DENSE_W)
            T0 = 2 * D0

            def gather(j):
                pe.wait_ge(s["pick_ready"], j + 1)
                for b in range(2):
                    o = bank_as(pB[:, 1 + b, :], 4, P)
                    for i in range(4):
                        k = 4 * b + i
                        for n, (a, src) in enumerate(((0, g_hi), (1, g_hi), (0, g_lo), (1, g_lo))):
                            ins = mm(o[:, i, :], src[:, a, P * k:P * (k + 1)], pick[:, a, :],
                                     start=(i == 0 and n == 0), stop=True, skip_group_check=True)
                    ins.then_inc(s["gather_psum"], 1)

            def slots(j):
                pe.wait_ge(s["choose_chain"], CHOOSE * j + CHOOSE)
                for a in range(A):
                    turn(B7[:, P * a:P * (a + 1)], pick[:, a, :].bitcast(F32), a == 0)
                for a in range(A):
                    ins = mm(B7[:, S:S + 1], pick[:, a, :].bitcast(F32), gcur[:, a:a + 1], start=False, stop=True,
                             skip_group_check=True)
                ins.then_inc(s["slot_psum"], 1)

            def scatter(j, half, last=False):
                pe.wait_ge(s["y_lo_done"], 2 * j + half + 1)
                if half and not last:
                    pe.wait_ge(s["added"], 4 * j + 2)
                for a in range(A):
                    o = pA[:, a, :] if last else pB[:, 1 + a, :]
                    for n, src in enumerate((y_hi, y_lo)):
                        ins = mm(o, spread[:, a, :], src[:, 512 * half:512 * (half + 1)], start=(n == 0), stop=(n == 1))
                    ins.then_inc(s["scatter_psum"], 1)

            def job(j, first=False, last=False):
                for kind, c, at, n in expert_order:
                    if kind == "gate":
                        pe.wait_ge(s["silu_done"], D0 + NCX * j + c)
                    if kind == "up":
                        pe.wait_ge(s["act_done"], D0 + NCX * j + c)
                    if kind == "down":
                        pe.wait_ge(s["aT_lo_done"], T0 + NCX * j + c + 1)
                        if c == 0 and not first:
                            pe.wait_ge(s["y_lo_done"], 2 * j)
                    for q in range(n):
                        m = EX0 + at + q
                        if kind == "gate" and c == 0 and q % 2 == 0:
                            pe.wait_ge(s["xg_lo_done"], 2 * j + q // 2 + 1)
                        if kind == "down":
                            row_piece(m, q, c == 0 and q == 0, [[B2, B3]], ex_hi[:, c % 2], ex_lo[:, c % 2], 1, j)
                        else:
                            chunk_piece(m, q, COLS, [B0 if kind == "gate" else B1], hT_hi, hT_lo, 1, j=j)
                        for cc, pos in te.items():
                            if pos == at + q:
                                pe.wait_ge(s["act_done"], D0 + NCX * j + cc + 1)
                                pe.wait_ge(s["aT_lo_done"], T0 + NCX * j + cc)
                                for k in range(4):
                                    ins = turn(B4[:, P * k:P * (k + 1)], ex_act[:, P * k:P * (k + 1)], k == 0)
                                ins.then_inc(s["aT_psum"], 1)
                        if at + q == 3 and not first:
                            scatter(j - 1, 0)
                        if at + q == 9 and not first:
                            scatter(j - 1, 1)
                        if at + q == 14:
                            slots(j)
                        if at + q == 71 and not last:
                            if not first:
                                pe.wait_ge(s["added"], 4 * j)
                            gather(j + 1)

            gather(0)
            job(0, first=True)
            middle = load_middle_jobs(pe)
            with pe.Fori(0, middle) as i:
                job(i + 1)
            job(middle + 1, last=True)
            pe.wait_ge(s["added"], 4 * middle + 4)
            scatter(middle + 1, 0)
            scatter(middle + 1, 1, last=True)

        @block.scalar
        def _(eng):
            f = nc.scalar.activation
            chain = [0]

            def link(ins):
                chain[0] += 1
                ins.then_inc(s["act_chain"], 1)
                eng.wait_ge(s["act_chain"], chain[0])

            nxt = [0]

            cap = [EX0 + FFE + AHEAD]

            def split_to(m_end, j=0):
                while nxt[0] < min(m_end, cap[0]):
                    m = nxt[0]
                    wait_loaded(eng, m, j)
                    if m >= PARTS:
                        eng.wait_ge(s["w_used"], piece_count(m - PARTS, j))
                    f(w_hi[:, m % PARTS, :], raw_slot(m),
                      ACT.Copy).then_inc(s["w_hi_done"], 1)
                    nxt[0] += 1

            def after(m, j=0):
                split_to(m + 1 + AHEAD, j)
                eng.wait_ge(s["w_used"], piece_count(m, j))

            def first_rms():
                eng.wait_ge(s["pads_ready"], 2)
                f(RMS[:, 0:1], one[:], ACT.Sqrt)
                for a in range(A):
                    eng.wait_ge(s[f"in_x{a}"], 16)
                    link(f(junk_v[:, a, :], x[:, a, :], ACT.Square, accum_out=SS[:, a:a + 1]))
                    f(RMS[:, a:a + 1], SS[:, a:a + 1], ACT.Sqrt, scale=1.0 / D, bias=eps[:]).then_inc(s["rms_ready"], 1)

            def rms_half(q, half):
                for a in range(A):
                    eng.wait_ge(s["x_ready"], 4 * (q - 1) + 2 * half + a + 1)
                    cols = slice(512 * half, 512 * (half + 1))
                    link(f(junk_v[:, a, cols], x[:, a, cols], ACT.Square, accum_out=SS[:, a:a + 1]))
                    if half == 0:
                        ins = f(SS0[:, a:a + 1], SS[:, a:a + 1], ACT.Identity, scale=1.0 / D, bias=eps[:])
                        if a == A - 1:
                            link(ins)
                            f(RMS, SS0, ACT.Sqrt)
                    else:
                        f(RMS[:, a:a + 1], SS[:, a:a + 1], ACT.Sqrt, scale=1.0 / D,
                          bias=SS0[:, a:a + 1]).then_inc(s["rms_ready"], 1)

            junk_v = xn_v

            def parts_hi(q, g_row):
                for b in range(4):
                    eng.wait_ge(s["xT_psum"], 4 * q + b + 1)
                    if q == 0 and b == 0:
                        eng.wait_ge(s["vec_ready"], 1)
                    for i in range(2):
                        k = 2 * b + i
                        ins = f(hT_hi[:, k, :], pB[:, b, S * i:S * (i + 1)], ACT.Copy, scale=col(g_row + k))
                    ins.then_inc(s["hT_hi_done"], 1)

            def narrow_hi(n, name):
                eng.wait_ge(s[name], 16)
                if n == 1:
                    eng.wait_ge(s["gate_psum"], 1)
                if n == 2:
                    eng.wait_ge(s["gate_psum"], 2)
                f(wg_hi[:], wg_raw[:], ACT.Copy).then_inc(s["wg_hi_done"], 1)

            def mixer(layer):
                m0 = M0[layer]
                if layer == 0:
                    narrow_hi(0, "in_wg0")
                parts_hi(2 * layer, R_MIXG + KT * layer)
                split_to(m0 + AHEAD)
                eng.wait_ge(s["gate_pre"], layer + 1)
                link(f(NABS, NABS, ACT.Exp))
                f(LN1, NABS, ACT.Ln, bias=one[:]).then_inc(s["soft_ready"], 1)
                for i in range(2):
                    after(m0 + 4 * i + 3)
                    f(conv_in[:, 4 * i:4 * i + 4, TAPS - 1:],
                      pA[:, 2 * i:2 * i + 2, :].rearrange("p b (f t) -> p (b f) t", f=2),
                      ACT.Copy).then_inc(s["lin_evac"], 1)
                split_to(m0 + 10 + AHEAD)
                eng.wait_ge(s["exp_args"], layer + 1)
                link(f(EARG, EARG, ACT.Exp))
                for a in range(A):
                    for h in range(MH):
                        ins = f(Wt[:, a, h, :], Wt[:, a, h, :], ACT.Exp, bias=NMU[:, MH * a + h:MH * a + h + 1])
                ins.then_inc(s["w_ready"], 1)
                after(m0 + 11)
                f(v[:], pA[:, 0:2, :], ACT.Copy).then_inc(s["lin_evac"], 1)
                after(m0 + 15)
                f(so[:], pA[:, 2:4, :], ACT.Sigmoid).then_inc(s["lin_evac"], 1)
                eng.wait_ge(s["conv_ready"], layer + 1)
                f(qk[:], qk[:], ACT.Silu).then_inc(s["qk_ready"], 1)
                after(m0 + 19)
                if layer == 0:
                    eng.wait_ge(s["brow_stored"], 16)
                f(aqk[:, 0], pA[:, 0:2, :], ACT.Copy).then_inc(s["lin_evac"], 1)
                after(m0 + 21)
                for a in range(A):
                    eng.wait_ge(s["sT_psum"], A * layer + a + 1)
                    f(sT[:, a], bank_as(pB[:, a, :], MH, P), ACT.Copy).then_inc(s["sT_ready"], 1)
                after(m0 + 23)
                f(aqk[:, 1], pA[:, 2:4, :], ACT.Copy).then_inc(s["lin_evac"], 1)
                eng.wait_ge(s["c_psum"], layer + 1)
                f(caug[:, :, 0:MD], bank_as(B6, MH, MD), ACT.Copy)
                f(caug[:, :, MD], B7[:, 0:MH], ACT.Copy).then_inc(s["c_ready"], 1)
                after(m0 + 24)
                eng.wait_ge(s["state_psum"], layer + 1)
                for h in range(MH):
                    o = pB[:, 2 + h // 2, (MD + 1) * (h % 2):(MD + 1) * (h % 2 + 1)]
                    ins = f(st_sb[:, h, :], o, ACT.Copy, scale=EARG[:, h:h + 1])
                ins.then_inc(s["state_ready"], 1)
                split_to(m0 + 26 + AHEAD)
                f(sq_v, aqk[:].rearrange("p w a n -> p (w a n)"), ACT.Square).then_inc(s["qkn_sq"], 1)
                eng.wait_ge(s["cell_ss"], layer + 1)
                f(CRMS, CSS, ACT.Sqrt, scale=1.0 / MD, bias=eps[:]).then_inc(s["cell_rms"], 1)
                split_to(m0 + 27 + AHEAD)
                eng.wait_ge(s["qkn_ss"], layer + 1)
                f(QRMS, QSS, ACT.Sqrt, scale=1.0 / AD, bias=eps[:]).then_inc(s["qkn_rms"], 1)
                after(m0 + 27)
                f(av[:], pA[:, 0:2, :], ACT.Copy).then_inc(s["lin_evac"], 1)
                split_to(m0 + 29 + AHEAD)
                for b in range(2):
                    eng.wait_ge(s["haT_psum"], 2 * layer + b + 1)
                    for i in range(2):
                        h = 2 * b + i
                        ins = f(haT_hi[:, h, :], pB[:, 2 + b, S * i:S * (i + 1)], ACT.Copy,
                                scale=col(R_MNG + MH * layer + h))
                    ins.then_inc(s["haT_hi_done"], 1)
                if layer == 0:
                    split_to(m0 + 31 + AHEAD)
                    eng.wait_ge(s["flip_psum"], 1)
                    f(toep[:].rearrange("p h j -> p (h j)"), pB[:].rearrange("p b c -> p (b c)"),
                      ACT.Copy).then_inc(s["toep_ready"], 1)
                split_to(m0 + 32 + AHEAD)
                for w, (dst, row) in enumerate(((qaT, R_QG), (kaT, R_KG))):
                    eng.wait_ge(s["qaT_psum"], 2 * layer + w + 1)
                    f(dst, pB[:, 2 * w:2 * w + 2, :].rearrange("p b (t c) -> p (b t) c", t=2), ACT.Copy,
                      scale=col(row + layer)).then_inc(s["qaT_ready"], 1)
                split_to(m0 + 34 + AHEAD)

                def gate(i):
                    after(m0 + 4 * i + 3)
                    i2 = i - 7
                    dst = ga if i2 < 2 else gb
                    f(dst[:, :, 512 * (i2 % 2):512 * (i2 % 2 + 1)], pA[:, 2 * (i % 2):2 * (i % 2) + 2, :],
                      ACT.Sigmoid).then_inc(s["lin_evac"], 1)

                for h in range(AH):
                    n = AH * layer + h
                    if h in (1, 5):
                        gate(7 + h // 4)
                    eng.wait_ge(s["L_ready"], n + 1)
                    for t, (c0, c1) in enumerate(((0, P), (P, P + S))):
                        ins = f(L[h % 2][:, c0:c1], L[h % 2][:, c0:c1], ACT.Exp, bias=MX[:, 2 * h + t:2 * h + t + 1],
                                accum_out=SUMS[:, 2 * h + t:2 * h + t + 1])
                    ins.then_inc(s["P_ready"], 1)
                    split_to(m0 + 35 + h + AHEAD)
                    eng.wait_ge(s["PT_psum"], n + 1)
                    if h >= 2:
                        eng.wait_ge(s["o_psum"], n - 1)
                    f(PT[h % 2], B6[:, 0:384], ACT.Copy).then_inc(s["PT_ready"], 1)
                gate(9)
                for b in range(2):
                    split_to(m0 + 43 + AHEAD)
                    eng.wait_ge(s["obT_psum"], 2 * layer + b + 1)
                    f(obT_hi[:, 2 * b:2 * b + 2, :], bank_as(pB[:, b, :], 2, S), ACT.Copy).then_inc(s["obT_hi_done"], 1)
                gate(10)
                split_to(m0 + 52 + AHEAD)
                for b in range(4):
                    if b == 2:
                        split_to(m0 + 54 + AHEAD)
                    eng.wait_ge(s["yT_psum"], 4 * layer + b + 1)
                    f(hT_hi[:, 2 * b:2 * b + 2, :], bank_as(pA[:, b, :], 2, S), ACT.Copy).then_inc(s["yT_hi"], 1)
                narrow_hi(layer + 1, f"in_wg{layer + 1}")
                after(m0 + MIX - 4)
                rms_half(2 * layer + 1, 0)
                after(m0 + MIX - 1)
                rms_half(2 * layer + 1, 1)

            eng.wait_ge(s["vec_zero"], 1)
            for r, src in ((R_QG, q_norm_g), (R_KG, k_norm_g)):
                for half in range(2):
                    eng.dma_start(vec_rows[r:r + NL, AD * half:AD * (half + 1)], src).then_inc(s["in_vec"], 16)
            eng.dma_start(wg_raw[:], w_in[0][:, G0:G0 + 8].rearrange("(k p) n -> p k n", p=P)).then_inc(s["in_wg0"], 16)
            first_rms()
            eng.wait_ge(s["vec_psum"], 1)
            f(vec[:], B4[:, 0:P], ACT.Copy).then_inc(s["vec_ready"], 1)
            mixer(0)

            parts_hi(1, R_FFNG)
            ta, en = turns(dense_order), ends(dense_order)
            for t in range(FFD):
                for c, w in enumerate(DENSE_W):
                    if t == en["gate", c]:
                        after(DN0 + t)
                        if c:
                            eng.wait_ge(s["act_done"], c)
                        f(sg[:, :, 0:w], pA[:, 0:2, 0:w], ACT.Silu).then_inc(s["silu_done"], 1)
                    if t == ta[c]:
                        after(DN0 + t)
                        for b in range(2):
                            eng.wait_ge(s["aT_psum"], 2 * c + b + 1)
                            k = w // COLS + 1
                            f(aT_hi[:, c % 2, k * b:k * (b + 1), :], bank_as(pA[:, 2 + b, :], k, S),
                              ACT.Copy).then_inc(s["aT_hi_done"], 1)
            split_to(DN0 + FFD + AHEAD)
            for half in range(2):
                after(DN0 + FFD - 2 + half)
                rms_half(2, half)

            mixer(1)

            parts_hi(3, R_FFNG + KT)
            for a in range(A):
                eng.wait_ge(s["xn_ready"], 8)
                ins = f(g_hi[:, a, :], xn_v[:, a, :], ACT.Copy)
            ins.then_inc(s["g_hi_done"], 1)
            split_to(EX0 + AHEAD)
            eng.wait_ge(s["route_exp"], 1)
            f(REXP, REXP, ACT.Exp).then_inc(s["route_sel"], 1)

            te, ee = turns(expert_order), ends(expert_order)
            NCX, D0 = len(EXPERT_W), len(DENSE_W)
            T0 = 2 * D0

            def gathered(j):
                for b in range(2):
                    eng.wait_ge(s["gather_psum"], 2 * j + b + 1)
                    for i in range(4):
                        k = 4 * b + i
                        ins = f(hT_hi[:, k, 0:P], pB[:, 1 + b, P * i:P * (i + 1)], ACT.Copy,
                                scale=col(R_FFNG + KT + k))
                    ins.then_inc(s["xg_hi_done"], 1)

            def output_hi(j):
                eng.wait_ge(s["slot_ready"], j + 1)
                for half in range(2):
                    f(y_hi[:, 512 * half:512 * (half + 1)], pA[:, 2 + half, :], ACT.Copy,
                      scale=gslot).then_inc(s["y_hi_done"], 1)

            def job(j, first=False, last=False):
                if last:
                    cap[0] = EX0 + FFE
                if not first:
                    output_hi(j - 1)
                for t in range(FFE):
                    for c in range(NCX):
                        if t == ee["gate", c]:
                            after(EX0 + t, j)
                            eng.wait_ge(s["act_done"], D0 + NCX * j + c)
                            f(ex_sg[:], B0, ACT.Silu).then_inc(s["silu_done"], 1)
                        if t == te[c]:
                            after(EX0 + t, j)
                            eng.wait_ge(s["aT_psum"], T0 + NCX * j + c + 1)
                            f(ex_hi[:, c % 2], bank_as(B4, 4, P), ACT.Copy).then_inc(s["aT_hi_done"], 1)
                    if t == 14:
                        split_to(EX0 + t + 1 + AHEAD, j)
                        eng.wait_ge(s["slot_psum"], j + 1)
                        if not first:
                            eng.wait_ge(s["y_lo_done"], 2 * j)
                        f(spread[:], bank_as(B7, A, P), ACT.Copy)
                        f(gslot, B7[:, S:S + 1], ACT.Copy).then_inc(s["slot_ready"], 1)
                    if t == 75 and not last:
                        after(EX0 + t, j)
                        gathered(j + 1)
                if not last:
                    after(EX0 + FFE - 1, j)
                    nxt[0] -= FFE
                else:
                    split_to(EX0 + FFE, j)
                    eng.wait_ge(s["w_used"], piece_count(EX0 + FFE - 1, j))
                    output_hi(j)

            gathered(0)
            job(0, first=True)
            middle = load_middle_jobs(eng)
            with eng.Fori(0, middle) as i:
                job(i + 1)
            job(middle + 1, last=True)

        @block.vector
        def _(eng):
            tt, ts, stt = nc.vector.tensor_tensor, nc.vector.tensor_scalar, nc.vector.scalar_tensor_tensor
            chain = [0]

            def link(ins):
                chain[0] += 1
                ins.then_inc(s["dve_chain"], 1)
                eng.wait_ge(s["dve_chain"], chain[0])

            nxt = [0]

            cap = [EX0 + FFE + AHEAD]

            def split_to(m_end, j=0):
                while nxt[0] < min(m_end, cap[0]):
                    m = nxt[0]
                    eng.wait_ge(s["w_hi_done"], piece_count(m, j))
                    tt(w_lo[:, m % PARTS, :], raw_slot(m),
                       w_hi[:, m % PARTS, :].bitcast(F32), ALU.subtract).then_inc(s["w_lo_done"], 1)
                    nxt[0] += 1

            def after(m, j=0):
                split_to(m + 1 + AHEAD, j)
                eng.wait_ge(s["w_used"], piece_count(m, j))

            def norm(q):
                for a in range(A):
                    eng.wait_ge(s["rms_ready"], A * q + a + 1)
                    link(nc.vector.reciprocal(RSTD[:, a:a + 1], RMS[:, a:a + 1]))
                    ts(xn_v[:, a, :], x[:, a, :], RSTD[:, a:a + 1], None, ALU.mult).then_inc(s["xn_ready"], 1)

            def parts_lo(q, g_row):
                for b in range(4):
                    eng.wait_ge(s["hT_hi_done"], 4 * q + b + 1)
                    for i in range(2):
                        k = 2 * b + i
                        ins = stt(hT_lo[:, k, :], pB[:, b, S * i:S * (i + 1)], col(g_row + k),
                                  hT_hi[:, k, :].bitcast(F32), ALU.mult, ALU.subtract)
                    ins.then_inc(s["hT_lo_done"], 1)

            def narrow_lo(n):
                eng.wait_ge(s["wg_hi_done"], n + 1)
                tt(wg_lo[:], wg_raw[:], wg_hi[:].bitcast(F32), ALU.subtract).then_inc(s["wg_lo_done"], 1)

            def narrow_rows(n):
                eng.wait_ge(s["narrow_psum"], n)
                nc.vector.tensor_copy(narrow_sb[:], B2[0:8, 0:S]).then_inc(s["narrow_rows"], 1)

            def mixer(layer):
                m0 = M0[layer]
                norm(2 * layer)
                if layer == 0:
                    narrow_lo(0)
                parts_lo(2 * layer, R_MIXG + KT * layer)
                narrow_rows(layer + 1)
                split_to(m0 + 2)
                eng.wait_ge(s["gate_psum"], layer + 1)
                if layer == 0:
                    eng.wait_ge(s["in_bias"], 16 * 7)
                pre = PRE.rearrange("p (a g) -> p a g", a=A)
                link(tt(pre, bank_as(B3, A, 8), gbias[:, layer:layer + 1, :].broadcast_to([P, A, 8]), ALU.add))
                ip, fp = pre[:, :, 0:MH], pre[:, :, MH:]
                v8 = [t.rearrange("p (a h) -> p a h", a=A) for t in (NABS, MINF, LF, BC, RR, RMAX, MU, DEN)]
                nabs, minf, lf, bc, rr, rmax, mu, den = v8
                ts(minf, fp, 0.0, None, ALU.min)
                stt(nabs, fp, -1.0, fp, ALU.mult, ALU.min).then_inc(s["gate_pre"], 1)
                eng.wait_ge(s["soft_ready"], layer + 1)
                tt(LF, MINF, LN1, ALU.subtract).then_inc(s["lf_ready"], 1)
                split_to(m0 + 4 + AHEAD)
                if layer == 0:
                    eng.wait_ge(s["brow_psum"], 1)
                    tt(brow_sb, B6[0:AH, 0:BT], bmask_sb, ALU.add).then_inc(s["brow_ready"], 1)
                eng.wait_ge(s["cum_psum"], layer + 1)
                link(nc.vector.tensor_copy(BC, B5[:, 0:8]))
                link(tt(rr, ip, bc, ALU.subtract))
                for a in range(A):
                    for h in range(MH):
                        ins = ts(Wt[:, a, h, :], ident, RR[:, MH * a + h:MH * a + h + 1], None, ALU.mult)
                ins.then_inc(s["diag_ready"], 1)
                split_to(m0 + 6 + AHEAD)
                eng.wait_ge(s["rb_psum"], layer + 1)
                for a in range(A):
                    link(tt(Wt[:, a], bank_as(pB[:, 2 + a, :], MH, P),
                            cst[:, CAUSAL:CAUSAL + 1, :].broadcast_to([P, MH, P]), ALU.add))
                    link(nc.vector.tensor_reduce(rmax[:, a, :], Wt[:, a], AX, ALU.max))
                link(ts(MU[:, 0:MH], RMAX[:, 0:MH], 0.0, None, ALU.max))
                link(nc.vector.tensor_copy(ST0[:, 0:MH], MU[:, 0:MH]))
                tt(ST0[:, MH:], MU[:, 0:MH], BC[:, 0:MH], ALU.add).then_inc(s["mu0_ready"], 1)
                split_to(m0 + 9 + AHEAD)
                eng.wait_ge(s["mulast_psum"], layer + 1)
                link(nc.vector.tensor_copy(MLAST, B7[:, 0:8]))
                link(tt(MU[:, MH:], RMAX[:, MH:], MLAST[:, MH:], ALU.max))
                link(ts(NMU, MU, -1.0, None, ALU.mult))
                tt(EARG[:, 0:MH], MLAST[:, MH:], MU[:, MH:], ALU.subtract)
                tt(EARG[:, MH:2 * MH], RR[:, 0:MH], MLAST[:, 0:MH], ALU.subtract)
                tt(EARG[:, 2 * MH:], NMU, BC, ALU.subtract).then_inc(s["exp_args"], 1)
                split_to(m0 + 10 + AHEAD)
                eng.wait_ge(s["lin_evac"], NCH * layer + 2)
                for t in range(2 * MH):
                    if t % 2 == 1:
                        split_to(m0 + 11 + t // 2 + AHEAD)
                    for tap in range(TAPS):
                        src = conv_in[:, t, tap:tap + S]
                        wc = col(R_CONVW + (layer * TAPS + tap) * KT + t)
                        if tap == 0:
                            link(ts(qk[:, t, :], src, wc, col(R_CONVB + layer * KT + t), ALU.mult, ALU.add))
                        else:
                            ins = stt(qk[:, t, :], src, wc, qk[:, t, :], ALU.mult, ALU.add)
                            if tap < TAPS - 1:
                                link(ins)
                ins.then_inc(s["conv_ready"], 1)
                after(m0 + 18)
                for a in range(A):
                    eng.wait_ge(s["w_ready"], layer + 1)
                    eng.wait_ge(s["qk_psum"], A * layer + a + 1)
                    link(stt(Wt[:, a], bank_as(pB[:, a, :], MH, P), float(MD) ** -0.5, Wt[:, a], ALU.mult, ALU.mult))
                    nc.vector.tensor_reduce(den[:, a, :], Wt[:, a], AX, ALU.add).then_inc(s["s_ready"], 1)
                eng.wait_ge(s["kt_psum"], layer + 1)
                for h in range(MH):
                    ins = ts(kw[:, h, :], B6[:, P * h:P * (h + 1)], EARG[:, MH + h:MH + h + 1], float(MD) ** -0.5,
                             ALU.mult, ALU.mult)
                ins.then_inc(s["kw_ready"], 1)
                split_to(m0 + 25 + AHEAD)
                expnm = EARG[:, 2 * MH:].rearrange("p (a h) -> p a h", a=A)
                for a in range(A):
                    if a == 1:
                        eng.wait_ge(s["state_ready"], layer + 1)
                        link(tt(den[:, 1, :], den[:, 1, :], st_sb[:, :, MD], ALU.add))
                    link(stt(den[:, a, :], den[:, a, :], -1.0, den[:, a, :], ALU.mult, ALU.max))
                    link(tt(den[:, a, :], den[:, a, :], expnm[:, a, :], ALU.max))
                    link(nc.vector.reciprocal(den[:, a, :], den[:, a, :]))
                    eng.wait_ge(s["num_psum"], A * layer + a + 1)
                    num = bank_as(pB[:, a, :], MH, MD)
                    h4 = Wt[:, a]
                    if a == 1:
                        link(tt(h4, num, st_sb[:, :, 0:MD], ALU.add))
                        num = h4
                    link(tt(h4, num, den[:, a, :].unsqueeze(2).broadcast_to([P, MH, MD]), ALU.mult))
                    if a == 0:
                        eng.wait_ge(s["lin_evac"], NCH * layer + 4)
                    so4 = so[:, a, :].rearrange("p (h d) -> p h d", h=MH)
                    link(tt(so4, so4, h4, ALU.mult))
                    link(tt(h4, so4, so4, ALU.mult))
                    ins = nc.vector.tensor_reduce(CSS[:, MH * a:MH * (a + 1)], h4, AX, ALU.add)
                    if a == 0:
                        link(ins)
                        split_to(m0 + 26 + AHEAD)
                ins.then_inc(s["cell_ss"], 1)
                split_to(m0 + 27 + AHEAD)
                eng.wait_ge(s["cell_rms"], layer + 1)
                link(nc.vector.reciprocal(CRMS, CRMS))
                sov = so[:].rearrange("p a (h d) -> p (a h) d", h=MH)
                tt(sov, sov, CRMS.unsqueeze(2).broadcast_to([P, A * MH, MD]), ALU.mult).then_inc(s["ha_ready"], 1)
                eng.wait_ge(s["qkn_sq"], layer + 1)
                nc.vector.tensor_reduce(QSS, sq_v.rearrange("p (b d) -> p b d", d=AD), AX, ALU.add)\
                    .then_inc(s["qkn_ss"], 1)
                split_to(m0 + 29 + AHEAD)
                for b in range(2):
                    eng.wait_ge(s["haT_hi_done"], 2 * layer + b + 1)
                    for i in range(2):
                        h = 2 * b + i
                        ins = stt(haT_lo[:, h, :], pB[:, 2 + b, S * i:S * (i + 1)], col(R_MNG + MH * layer + h),
                                  haT_hi[:, h, :].bitcast(F32), ALU.mult, ALU.subtract)
                    ins.then_inc(s["haT_lo_done"], 1)
                eng.wait_ge(s["qkn_rms"], layer + 1)
                link(nc.vector.reciprocal(QRMS, QRMS))
                qkh = aqk[:].rearrange("p w a (h d) -> p (w a h) d", h=AH)
                tt(qkh, qkh, QRMS.unsqueeze(2).broadcast_to([P, 4 * AH, AD]), ALU.mult).then_inc(s["qkn_ready"], 1)
                split_to(m0 + 34 + AHEAD)
                for h in range(AH):
                    n = AH * layer + h
                    split_to(m0 + min(34 + max(h - 1, 0), 41) + AHEAD)
                    eng.wait_ge(s["lg_psum"], n + 1)
                    if h >= 2:
                        eng.wait_ge(s["PT_psum"], n - 1)
                    o, l = pB[:, h % 2, :], L[h % 2]
                    stt(l[:, 0:P], o[:, 0:P], float(AD) ** -0.5, toep[:, h, P:S], ALU.mult, ALU.add)
                    link(stt(l[:, P:P + S], o[:, P:P + S], float(AD) ** -0.5, toep[:, h, :], ALU.mult, ALU.add))
                    nc.vector.tensor_reduce(MX[:, 2 * h:2 * h + 1], l[:, 0:P], AX, ALU.max)
                    link(nc.vector.tensor_reduce(MX[:, 2 * h + 1:2 * h + 2], l[:, P:P + S], AX, ALU.max))
                    ts(MX[:, 2 * h:2 * h + 2], MX[:, 2 * h:2 * h + 2], -1.0, None, ALU.mult).then_inc(s["L_ready"], 1)
                    if h == 5 or h == 7:
                        q = h // 6
                        if q:
                            split_to(m0 + 42 + AHEAD)
                        eng.wait_ge(s["o_psum"], AH * layer + 4 * q + 4)
                        sums = SUMS[:, 8 * q:8 * q + 8]
                        link(nc.vector.reciprocal(sums, sums))
                        o4 = bank_as(B7, A, 4, AD)
                        for a in range(A):
                            r = sums.rearrange("p (h a) -> p a h", a=A)[:, a, :].unsqueeze(2).broadcast_to([P, 4, AD])
                            dst = ob[:, a, 4 * AD * q:4 * AD * (q + 1)].rearrange("p (h d) -> p h d", h=4)
                            ins = tt(dst, o4[:, a], r, ALU.mult)
                        ins.then_inc(s["o_evac"], 1)
                split_to(m0 + 43 + AHEAD)
                for b in range(2):
                    eng.wait_ge(s["obT_hi_done"], 2 * layer + b + 1)
                    tt(obT_lo[:, 2 * b:2 * b + 2, :], bank_as(pB[:, b, :], 2, S),
                       obT_hi[:, 2 * b:2 * b + 2, :].bitcast(F32), ALU.subtract).then_inc(s["obT_lo_done"], 1)
                eng.wait_ge(s["lin_evac"], NCH * (layer + 1))

                def part(t, a, half):
                    return t[:, a, 512 * half:512 * (half + 1)]

                for half in range(2):
                    after(m0 + 45 + 2 * half)
                    for a in range(A):
                        ins = tt(part(ga, a, half), halves(pA, half)[a], part(ga, a, half), ALU.mult)
                link(ins)
                after(m0 + 49)
                for a in range(A):
                    link(tt(part(gb, a, 0), halves(pB, 0)[a], part(gb, a, 0), ALU.mult))
                    ins = tt(part(ga, a, 0), part(ga, a, 0), part(gb, a, 0), ALU.add)
                ins.then_inc(s["y_ready"], 1)
                after(m0 + 51)
                for a in range(A):
                    ins = tt(part(gb, a, 1), halves(pB, 1)[a], part(gb, a, 1), ALU.mult)
                link(ins)
                for b in range(4):
                    if b == 2:
                        for a in range(A):
                            ins = tt(part(ga, a, 1), part(ga, a, 1), part(gb, a, 1), ALU.add)
                        ins.then_inc(s["y_ready"], 1)
                        split_to(m0 + 54 + AHEAD)
                    eng.wait_ge(s["yT_hi"], 4 * layer + b + 1)
                    tt(hT_lo[:, 2 * b:2 * b + 2, :], bank_as(pA[:, b, :], 2, S),
                       hT_hi[:, 2 * b:2 * b + 2, :].bitcast(F32), ALU.subtract).then_inc(s["h_parts"], 1)
                narrow_lo(layer + 1)
                for half in range(2):
                    after(m0 + MIX - 5 + 4 * half)
                    add_banks(half)

            def halves(p4, half):
                return [p4[:, 2 * (1 - half) + a, :] for a in range(A)]

            def add_banks(half):
                for a in range(A):
                    y = x[:, a, 512 * half:512 * (half + 1)]
                    tt(y, halves(pB, half)[a], y, ALU.add).then_inc(s["x_ready"], 1)

            nc.vector.memset(vec_rows, 0.0).then_inc(s["vec_zero"], 1)
            link(nc.vector.memset(conv_in[:, :, 0:TAPS - 1], 0.0))
            mixer(0)

            norm(1)
            parts_lo(1, R_FFNG)
            ta, en = turns(dense_order), ends(dense_order)
            for t in range(FFD):
                for c, w in enumerate(DENSE_W):
                    if t == en["up", c]:
                        after(DN0 + t)
                        eng.wait_ge(s["silu_done"], c + 1)
                        if c:
                            eng.wait_ge(s["aT_psum"], 2 * c)
                        for a in range(A):
                            ins = tt(act[:, a, 0:w], pA[:, 2 + a, 0:w], sg[:, a, 0:w], ALU.mult)
                        ins.then_inc(s["act_done"], 1)
                    if t == ta[c]:
                        after(DN0 + t)
                        for b in range(2):
                            k = w // COLS + 1
                            eng.wait_ge(s["aT_hi_done"], 2 * c + b + 1)
                            tt(aT_lo[:, c % 2, k * b:k * (b + 1), :], bank_as(pA[:, 2 + b, :], k, S),
                               aT_hi[:, c % 2, k * b:k * (b + 1), :].bitcast(F32), ALU.subtract)\
                                .then_inc(s["aT_lo_done"], 1)
            split_to(DN0 + FFD + AHEAD)
            for half in range(2):
                after(DN0 + FFD - 2 + half)
                add_banks(half)
            eng.wait_ge(s["x_ready"], 8)
            link(nc.vector.memset(conv_in[:, :, 0:TAPS - 1], 0.0))

            mixer(1)

            norm(3)
            parts_lo(3, R_FFNG + KT)
            narrow_rows(3)
            eng.wait_ge(s["logit_psum"], 1)
            iota = cst[:, IOTA, 0:NE]
            iota_b = cst[:, IOTA:IOTA + 1, 0:NE].broadcast_to([P, A, NE])
            lg = sm(8, 16).rearrange("p (a e) -> p a e", a=A)
            t1, hot1, hot2 = [sm(c, 16).rearrange("p (a e) -> p a e", a=A) for c in (24, 40, 56)]
            m1, m2, idx = sm(72, A), sm(74, A), sm(76, A)

            def wide(t):
                return t.unsqueeze(2).broadcast_to([P, A, NE])

            def top(m, hot):
                link(nc.vector.tensor_reduce(m, lg, AX, ALU.max))
                link(tt(t1, lg, wide(m), ALU.is_equal))
                link(stt(t1, t1, -8.0, iota_b, ALU.mult, ALU.add))
                link(nc.vector.tensor_reduce(idx, t1, AX, ALU.min))
                link(stt(hot, iota_b, -8.0, wide(idx), ALU.add, ALU.is_equal))

            link(nc.vector.tensor_copy(lg, bank_as(B3, A, 8)))
            top(m1, hot1)
            link(stt(lg, hot1, NEG, lg, ALU.mult, ALU.add))
            top(m2, hot2)
            tt(REXP, m2, m1, ALU.subtract).then_inc(s["route_exp"], 1)
            sel = sel_v
            tt(sel, hot1, hot2, ALU.add).then_inc(s["sel_ready"], 1)
            eng.wait_ge(s["g_hi_done"], 1)
            for a in range(A):
                tt(g_lo[:, a, :], xn_v[:, a, :], g_hi[:, a, :].bitcast(F32), ALU.subtract)

            def gate_table():
                count_jobs()
                eng.wait_ge(s["route_sel"], 1)
                link(ts(m1, REXP, 1.0, None, ALU.add))
                link(nc.vector.reciprocal(m1, m1))
                link(tt(m2, m1, REXP, ALU.mult))
                link(tt(hot1, hot1, wide(m1), ALU.mult))
                link(tt(hot2, hot2, wide(m2), ALU.mult))
                for r in range(ROUNDS):
                    link(tt(gates[:, :, NE * r:NE * (r + 1)], hot1, hot2, ALU.add))

            eng.wait_ge(s["rank_psum"], 1)
            link(stt(t1, bank_as(B5, A, 8), 1.0, sel, ALU.add, ALU.mult))
            nc.vector.tensor_reduce(idx[:, 0:1], B5[:, 16:24], AX, ALU.max)
            nc.vector.memset(jcount, 0.0)
            for r in range(ROUNDS):
                ins = ts(keys[:, :, NE * r:NE * (r + 1)], t1, -1.0 - P * r, None, ALU.add)
            link(ins)

            def count_jobs():
                link(ts(idx[:, 0:1], idx[:, 0:1], P + 0.5, float(JOBS - NE), ALU.is_gt, ALU.mult))
                ts(middle_jobs[:], idx[:, 0:1], NE - 2.0, None, ALU.add).then_inc(s["middle_ready"], 1)

            def choose(j, before_gates=None):
                hj = sm(104, JOBS)
                prod = sm(120, A * JOBS).rearrange("p (a e) -> p a e", a=A)
                hw = hj.unsqueeze(1).broadcast_to([P, A, JOBS])
                ch = [0]

                def lk(ins):
                    ch[0] += 1
                    ins.then_inc(s["choose_chain"], 1)
                    eng.wait_ge(s["choose_chain"], CHOOSE * j + ch[0])

                lk(ts(hj, cst[:, IOTA, 0:JOBS], jcount, None, ALU.is_equal))
                lk(ts(jcount, jcount, 1.0, None, ALU.add))
                lk(tt(prod, keys[:], hw, ALU.mult))
                lk(nc.vector.tensor_reduce(kcur, prod, AX, ALU.add))
                for a in range(A):
                    ins = ts(pick[:, a, :], cst[:, IOTA, :], kcur[:, a:a + 1], None, ALU.is_equal)
                ins.then_inc(s["pick_ready"], 1)
                if before_gates:
                    before_gates()
                lk(tt(prod, gates[:], hw, ALU.mult))
                lk(nc.vector.tensor_reduce(gcur, prod, AX, ALU.add))
                assert ch[0] == CHOOSE

            te, ee = turns(expert_order), ends(expert_order)
            NCX, D0 = len(EXPERT_W), len(DENSE_W)
            T0 = 2 * D0

            def gathered(j):
                for b in range(2):
                    eng.wait_ge(s["xg_hi_done"], 2 * j + b + 1)
                    for i in range(4):
                        k = 4 * b + i
                        ins = stt(hT_lo[:, k, 0:P], pB[:, 1 + b, P * i:P * (i + 1)], col(R_FFNG + KT + k),
                                  hT_hi[:, k, 0:P].bitcast(F32), ALU.mult, ALU.subtract)
                    ins.then_inc(s["xg_lo_done"], 1)

            def output_lo(j):
                for half in range(2):
                    cols = slice(512 * half, 512 * (half + 1))
                    eng.wait_ge(s["y_hi_done"], 2 * j + half + 1)
                    stt(y_lo[:, cols], pA[:, 2 + half, :], gslot, y_hi[:, cols].bitcast(F32),
                        ALU.mult, ALU.subtract).then_inc(s["y_lo_done"], 1)

            def add_half(j, half, last=False):
                for a in range(A):
                    eng.wait_ge(s["scatter_psum"], 4 * j + 2 * half + a + 1)
                    y = x[:, a, 512 * half:512 * (half + 1)]
                    tt(y, pA[:, a, :] if last else pB[:, 1 + a, :], y, ALU.add).then_inc(s["added"], 1)

            def job(j, first=False, last=False):
                if last:
                    cap[0] = EX0 + FFE
                if not first:
                    output_lo(j - 1)
                for t in range(FFE):
                    for c in range(NCX):
                        if t == ee["up", c]:
                            after(EX0 + t, j)
                            eng.wait_ge(s["silu_done"], D0 + NCX * j + c + 1)
                            eng.wait_ge(s["aT_psum"], T0 + NCX * j + c)
                            tt(ex_act[:], B1, ex_sg[:], ALU.mult).then_inc(s["act_done"], 1)
                        if t == te[c]:
                            after(EX0 + t, j)
                            eng.wait_ge(s["aT_hi_done"], T0 + NCX * j + c + 1)
                            tt(ex_lo[:, c % 2], bank_as(B4, 4, P), ex_hi[:, c % 2].bitcast(F32),
                               ALU.subtract).then_inc(s["aT_lo_done"], 1)
                    if t in (3, 10) and not first:
                        split_to(EX0 + t + 1 + AHEAD, j)
                        add_half(j - 1, t // 10)
                    if t == 20 and not last:
                        after(EX0 + t, j)
                        eng.wait_ge(s["slot_psum"], j + 1)
                        choose(j + 1)
                    if t == 75 and not last:
                        after(EX0 + t, j)
                        gathered(j + 1)
                if not last:
                    after(EX0 + FFE - 1, j)
                    nxt[0] -= FFE
                else:
                    split_to(EX0 + FFE, j)
                    output_lo(j)
                    add_half(j, 0)
                    add_half(j, 1, last=True)

            choose(0, gate_table)
            split_to(EX0 + AHEAD)
            gathered(0)
            job(0, first=True)
            middle = load_middle_jobs(eng)
            with eng.Fori(0, middle) as i:
                job(i + 1)
            job(middle + 1, last=True)


def tables():
    import numpy as np

    r = np.arange(P)
    c = np.zeros((P, 8, P), np.float32)
    c[:, IDENT] = r[:, None] == r
    c[:, TRIU] = r[:, None] <= r
    c[:, STRICT] = r[:, None] < r
    c[P - 1, LAST] = 1
    c[:, FLIP] = r[:, None] == P - 1 - r
    c[:, CAUSAL] = np.where(r[:, None] >= r, 0, NEG)
    c[:, IOTA] = r
    c[:, ONES] = 1
    buckets, exact, furthest = 32, 16, 1024
    n = (S - 1 - np.arange(BT)).clip(0)
    ratio = np.log(np.maximum(n, exact).astype(np.float32) / np.float32(exact)) / np.float32(np.log(furthest / exact))
    large = np.minimum(exact + (ratio * np.float32(buckets - exact)).astype(np.int32), buckets - 1)
    bucket = np.where(n < exact, n, large)
    past = np.arange(BT) < S
    hot = ((np.arange(buckets)[:, None] == bucket) & past).astype(np.float32)
    mask = np.broadcast_to(np.where(past, 0, NEG).astype(np.float32), (AH, BT)).copy()
    return c.reshape(P, 8 * P), hot, mask


_INS = ["x", "rel_bias", "mix_norm_g", "w_in", "conv_w", "conv_b", "igate_b", "fgate_b", "mlstm_norm_g",
        "q_norm_g", "k_norm_g", "w_branch_a", "w_branch_b", "w_out", "ffn_norm_g", "dense_w_gate", "dense_w_up",
        "dense_w_down", "router_w", "expert_w_gate", "expert_w_up", "expert_w_down"]


def kernel(**inputs):
    import numpy as np
    import concourse.bacc as bacc
    from concourse.bass_utils import run_bass_kernel_spmd as run

    nc = bacc.Bacc("TRN2", target_bir_lowering=False, num_devices=1)
    arrays = {f"{n}_dram": np.ascontiguousarray(inputs[n]) for n in _INS}
    arrays.update(zip(("consts_dram", "bucket_hot_dram", "bucket_mask_dram"), tables()))
    args = [nc.dram_tensor(n, a.shape, mybir.dt.from_np(a.dtype), kind="ExternalInput").ap()
            for n, a in arrays.items()]
    args.append(nc.dram_tensor("bias_rows_dram", (AH, BT), F32, kind="Internal").ap())
    args.append(nc.dram_tensor("out_dram", (1, S, D), F32, kind="ExternalOutput").ap())
    program(nc, *args)
    return run(nc, [arrays], core_ids=[0]).results[0]["out_dram"]
```
